# Optimizing a Trainium2 kernel written in Bass

```python
import jax, jax.numpy as jnp
from jax import lax
import numpy as np

D_MODEL = 1024
BATCH = 1
SEQ = 128
DEPTH = 2
DEC_BATCH = 1
DEC_SEQ = 128
PAST_LEN = 128

GRID_W = 64
MA_HEADS = 4
MA_DK = 128
MA_DV = 128
MA_CHUNK = 64
NA_HEADS = 8
NA_DH = 64
NA_KR_MAX = 8
NA_KC = 16
NA_QB = 16
NA_KB = NA_QB + NA_KC
CTX_QBLOCK = 128
HG_HEADS = 4
HG_DK = 128
HG_DV = 128
HG_CHUNK = 32
BRANCH_W = 512
MA_W = MA_HEADS * MA_DK
NA_W = NA_HEADS * NA_DH
HG_W = HG_HEADS * HG_DK
N_GROUPS = 4
EXP_PER_GROUP = 4
N_EXPERTS = N_GROUPS * EXP_PER_GROUP
TOP_K_INNER = 2
D_EXPERT = 512
ROPE_BASE = 10000.0
LN_EPS = 1e-5
RMS_EPS = 1e-6
DEEPNORM_ALPHA = (2 * DEPTH) ** 0.25
DEEPNORM_BETA = (8 * DEPTH) ** -0.25
IN_SIZES = (MA_W, MA_W, MA_HEADS * MA_DV, MA_HEADS * MA_DV,
            MA_HEADS, MA_HEADS, MA_HEADS, MA_HEADS,
            NA_W, NA_W, NA_W,
            HG_W, HG_W, HG_W, HG_HEADS * HG_DV, HG_HEADS * HG_DV,
            D_MODEL, D_MODEL, D_MODEL)
N_IN = sum(IN_SIZES)

kernel_name = "hybrid_mlstm_natten_hgrn2_hmoe_diffusion_step"

def layer_norm(x, g, b):
    xf = x.astype(jnp.float32)
    mu = jnp.mean(xf, -1, keepdims=True)
    var = jnp.mean(jnp.square(xf - mu), -1, keepdims=True)
    return ((xf - mu) * lax.rsqrt(var + LN_EPS)).astype(x.dtype) * g + b

def split_heads(a, n):
    B_, T_, W_ = a.shape
    return a.reshape(B_, T_, n, W_ // n).transpose(0, 2, 1, 3)

def merge_heads(a):
    B_, n, T_, d = a.shape
    return a.transpose(0, 2, 1, 3).reshape(B_, T_, n * d)

def flip_t(a):
    return jnp.flip(a, axis=2)

def to_chunks(a, L):
    B_, H_, T_ = a.shape[:3]
    return jnp.moveaxis(a.reshape(B_, H_, T_ // L, L, *a.shape[3:]), 2, 0)

def from_chunks(a):
    a = jnp.moveaxis(a, 0, 2)
    return a.reshape(a.shape[0], a.shape[1], -1, *a.shape[4:])

def axial_rope(x):
    T_ = x.shape[2]
    t = jnp.arange(T_)
    row = (t // GRID_W).astype(jnp.float32)
    col = (t % GRID_W).astype(jnp.float32)
    half = x.shape[-1] // 2
    inv = ROPE_BASE ** (-jnp.arange(0, half, 2, dtype=jnp.float32) / half)

    def rot(xp, pos):
        ang = pos[:, None] * inv[None, :]
        cos, sin = jnp.cos(ang).astype(x.dtype), jnp.sin(ang).astype(x.dtype)
        x1, x2 = xp[..., :half // 2], xp[..., half // 2:]
        return jnp.concatenate([x1 * cos - x2 * sin, x1 * sin + x2 * cos], -1)

    return jnp.concatenate([rot(x[..., :half], row), rot(x[..., half:], col)], -1)

def mlstm_chunkwise(q, k, v, ig, lf, C0, n0, m0):
    f32 = jnp.float32
    L = MA_CHUNK
    causal = jnp.tril(jnp.ones((L, L), bool))

    def step(carry, inp):
        C, n, m = carry
        qc, kc, vc, ic, fc = inp
        b = jnp.cumsum(fc, axis=-1)
        dmat = jnp.where(causal, b[..., :, None] - b[..., None, :] + ic[..., None, :], -jnp.inf)
        g = b + m[..., None]
        m_t = jnp.maximum(g, jnp.max(dmat, -1))
        w_inter = jnp.exp(g - m_t)
        s = jnp.einsum('bhtd,bhsd->bhts', qc, kc) * jnp.exp(dmat - m_t[..., None])
        num = w_inter[..., None] * jnp.einsum('bhtd,bhde->bhte', qc, C) + jnp.einsum('bhts,bhse->bhte', s, vc)
        den = w_inter * jnp.einsum('bhtd,bhd->bht', qc, n) + jnp.sum(s, -1)
        h = num / jnp.maximum(jnp.abs(den), jnp.exp(-m_t))[..., None]
        m_new = m_t[..., -1]
        decay_state = jnp.exp(b[..., -1] + m - m_new)
        kw = kc * jnp.exp(b[..., -1:] - b + ic - m_new[..., None])[..., None]
        C_new = decay_state[..., None, None] * C + jnp.einsum('bhsd,bhse->bhde', kw, vc)
        n_new = decay_state[..., None] * n + jnp.sum(kw, -2)
        return (C_new, n_new, m_new), h

    xs = (to_chunks(q, L), to_chunks(k, L), to_chunks(v, L), to_chunks(ig, L), to_chunks(lf, L))
    (C, n, m), hs = lax.scan(step, (C0.astype(f32), n0.astype(f32), m0.astype(f32)), xs)
    return from_chunks(hs), C, n, m

def hgrn2_chunkwise(q, k, i, logf, S0):
    L = HG_CHUNK
    causal = jnp.tril(jnp.ones((L, L), bool))[:, :, None]

    def step(S, inp):
        qc, kc, ic, lc = inp
        A = jnp.cumsum(lc, axis=2)
        o_inter = jnp.einsum('bhtd,bhde->bhte', qc * jnp.exp(A), S)
        diff = jnp.where(causal, A[:, :, :, None, :] - A[:, :, None, :, :], -jnp.inf)
        att = jnp.einsum('bhtd,bhtsd,bhsd->bhts', qc, jnp.exp(diff), kc)
        o = o_inter + jnp.einsum('bhts,bhse->bhte', att, ic)
        A_last = A[:, :, -1]
        S_new = jnp.exp(A_last)[..., None] * S + jnp.einsum('bhsd,bhse->bhde', kc * jnp.exp(A_last[:, :, None] - A), ic)
        return S_new, o

    xs = (to_chunks(q, L), to_chunks(k, L), to_chunks(i, L), to_chunks(logf, L))
    S, os_ = lax.scan(step, S0.astype(jnp.float32), xs)
    return from_chunks(os_), S

def context_attention(q, k, v):
    B_, H_, S_, D_ = q.shape
    nb = S_ // CTX_QBLOCK
    qb = jnp.moveaxis(q.reshape(B_, H_, nb, CTX_QBLOCK, D_), 2, 0)

    def one(qblk):
        s = jnp.einsum('bhqd,bhkd->bhqk', qblk, k).astype(jnp.float32)
        p = jax.nn.softmax(s, axis=-1).astype(v.dtype)
        return jnp.einsum('bhqk,bhkd->bhqd', p, v)

    o = lax.map(one, qb)
    return jnp.moveaxis(o, 0, 2).reshape(B_, H_, S_, D_)

def latent_neighbourhood_attention(q, k, v, ck, cv, rpb):
    B_, H_, T_, D_ = q.shape
    rows = T_ // GRID_W
    kr = min(NA_KR_MAX, rows)
    nj = GRID_W // NA_QB
    qcol = np.arange(GRID_W)
    c0 = np.clip(qcol - NA_KC // 2, 0, GRID_W - NA_KC)
    cb = np.clip(np.arange(nj) * NA_QB - NA_KC // 2, 0, GRID_W - NA_KB)
    col_idx = cb[:, None] + np.arange(NA_KB)[None, :]
    kcol = col_idx[:, None, :]
    c0b = c0.reshape(nj, NA_QB)[:, :, None]
    col_mask = (kcol >= c0b) & (kcol < c0b + NA_KC)
    dc_idx = np.clip(kcol - qcol.reshape(nj, NA_QB)[:, :, None] + NA_KC - 1, 0, 2 * NA_KC - 2)
    rpb_cols = rpb[:, :, dc_idx]
    kg = k.reshape(B_, H_, rows, GRID_W, D_)
    vg = v.reshape(B_, H_, rows, GRID_W, D_)
    q_rows = jnp.moveaxis(q.reshape(B_, H_, rows, nj, NA_QB, D_), 2, 0)
    n_loc = kr * NA_KB

    def one_row(args):
        r, qr = args
        r0 = jnp.clip(r - kr // 2, 0, rows - kr)
        ks = lax.dynamic_slice_in_dim(kg, r0, kr, axis=2)[:, :, :, col_idx]
        vs = lax.dynamic_slice_in_dim(vg, r0, kr, axis=2)[:, :, :, col_idx]
        dr_idx = r0 + jnp.arange(kr) - r + (NA_KR_MAX - 1)
        bias = jnp.transpose(jnp.take(rpb_cols, dr_idx, axis=1), (0, 2, 3, 1, 4)).astype(jnp.float32)
        s_loc = jnp.einsum('bhjqd,bhrjkd->bhjqrk', qr, ks).astype(jnp.float32) + bias
        s_loc = jnp.where(col_mask[:, :, None, :], s_loc, -jnp.inf)
        s_ctx = jnp.einsum('bhjqd,bhpd->bhjqp', qr, ck).astype(jnp.float32)
        s = jnp.concatenate([s_loc.reshape(B_, H_, nj, NA_QB, n_loc), s_ctx], -1)
        p = jax.nn.softmax(s, axis=-1).astype(v.dtype)
        p_loc = p[..., :n_loc].reshape(B_, H_, nj, NA_QB, kr, NA_KB)
        return jnp.einsum('bhjqrk,bhrjkd->bhjqd', p_loc, vs) + jnp.einsum('bhjqp,bhpd->bhjqd', p[..., n_loc:], cv)

    out = lax.map(one_row, (jnp.arange(rows), q_rows))
    return jnp.moveaxis(out, 0, 2).reshape(B_, H_, T_, D_)

def token_mixing(h, latent, mC0, mn0, mm0, hS0, ctx_k, ctx_v,
                 w_in_l, b_in_l, fbias_l, lb_l, rpb_l, w_branch_l, w_out_l):
    f32 = jnp.float32
    idx = np.cumsum(np.array(IN_SIZES))[:-1].tolist()
    (aq, ak, av, ao, ai_f, af_f, ai_b, af_b, bq, bk, bv,
     cf_f, cf_b, cq, ci, cg, ga, gb, gc) = jnp.split(h @ w_in_l + b_in_l, idx, axis=-1)
    q = split_heads(aq, MA_HEADS)
    k = split_heads(ak, MA_HEADS) * (MA_DK ** -0.5)
    v = split_heads(av, MA_HEADS)
    if latent:
        q, k = axial_rope(q), axial_rope(k)
    q, k, v = q.astype(f32), k.astype(f32), v.astype(f32)
    fb = fbias_l.astype(f32)
    ig_f = jnp.swapaxes(ai_f, 1, 2).astype(f32)
    ig_b = jnp.swapaxes(ai_b, 1, 2).astype(f32)
    lf_f = jax.nn.log_sigmoid(jnp.swapaxes(af_f, 1, 2).astype(f32) + fb[0][:, None])
    lf_b = jax.nn.log_sigmoid(jnp.swapaxes(af_b, 1, 2).astype(f32) + fb[1][:, None])
    hf, Cf, nf, mf = mlstm_chunkwise(q, k, v, ig_f, lf_f, mC0[:, 0], mn0[:, 0], mm0[:, 0])
    hb, Cb, nb_, mb = mlstm_chunkwise(flip_t(q), flip_t(k), flip_t(v), flip_t(ig_b), flip_t(lf_b),
                                      mC0[:, 1], mn0[:, 1], mm0[:, 1])
    a_out = merge_heads(jax.nn.sigmoid(split_heads(ao, MA_HEADS).astype(f32)) * (hf + flip_t(hb))).astype(h.dtype)
    nq = split_heads(bq, NA_HEADS) * (NA_DH ** -0.5)
    nk = split_heads(bk, NA_HEADS)
    nv = split_heads(bv, NA_HEADS)
    if latent:
        b_heads = latent_neighbourhood_attention(nq, nk, nv, ctx_k, ctx_v, rpb_l)
    else:
        b_heads = context_attention(nq, nk, nv)
        ctx_k, ctx_v = nk, nv
    b_out = merge_heads(b_heads)
    f_f = lb_l[0] + (1.0 - lb_l[0]) * jax.nn.sigmoid(cf_f.astype(f32))
    f_b = lb_l[1] + (1.0 - lb_l[1]) * jax.nn.sigmoid(cf_b.astype(f32))
    f_f, f_b = split_heads(f_f, HG_HEADS), split_heads(f_b, HG_HEADS)
    hq = split_heads(jax.nn.silu(cq.astype(f32)), HG_HEADS)
    hi = split_heads(ci.astype(f32), HG_HEADS)
    of, Sf = hgrn2_chunkwise(hq, 1.0 - f_f, hi, jnp.log(f_f), hS0[:, 0])
    ob, Sb = hgrn2_chunkwise(flip_t(hq), flip_t(1.0 - f_b), flip_t(hi), flip_t(jnp.log(f_b)), hS0[:, 1])
    o = of + flip_t(ob)
    o = o * lax.rsqrt(jnp.mean(o * o, -1, keepdims=True) + RMS_EPS)
    c_out = (merge_heads(o) * jax.nn.silu(cg.astype(f32))).astype(h.dtype)
    y = (jax.nn.sigmoid(ga) * (a_out @ w_branch_l[0])
         + jax.nn.sigmoid(gb) * (b_out @ w_branch_l[1])
         + jax.nn.sigmoid(gc) * (c_out @ w_branch_l[2])) @ w_out_l
    if latent:
        return y, None
    states = (ctx_k, ctx_v, jnp.stack([Cf, Cb], 1), jnp.stack([nf, nb_], 1),
              jnp.stack([mf, mb], 1), jnp.stack([Sf, Sb], 1))
    return y, states

def hier_moe(h, w_rg_l, w_re_l, w_e1_l, w_e3_l, w_e2_l):
    f32 = jnp.float32
    B_, T_, D_ = h.shape
    x = h.reshape(-1, D_)
    lg = (x @ w_rg_l).astype(f32)
    g_sel = jnp.argmax(lg, -1)
    p_sel = jnp.take_along_axis(jax.nn.softmax(lg, -1), g_sel[:, None], -1)
    le = (x @ w_re_l).astype(f32).reshape(-1, N_GROUPS, EXP_PER_GROUP)
    le_sel = jnp.take_along_axis(le, g_sel[:, None, None], 1)[:, 0]
    top_v, top_i = lax.top_k(le_sel, TOP_K_INNER)
    w_top = jax.nn.softmax(top_v, -1) * p_sel
    expert_id = g_sel[:, None] * EXP_PER_GROUP + top_i
    gate = jnp.einsum('nk,nke->ne', w_top, jax.nn.one_hot(expert_id, N_EXPERTS, dtype=f32))
    hid = jax.nn.silu(jnp.einsum('nd,edf->nef', x, w_e1_l)) * jnp.einsum('nd,edf->nef', x, w_e3_l)
    y = jnp.einsum('nef,efd->nd', hid * gate.astype(x.dtype)[..., None], w_e2_l)
    return y.reshape(B_, T_, D_)

def trunk_layer(x, mod, latent, mC0, mn0, mm0, hS0, ctx_k, ctx_v,
                w_in_l, b_in_l, fbias_l, lb_l, rpb_l, w_branch_l, w_out_l,
                ln_g_l, ln_b_l, w_rg_l, w_re_l, w_e1_l, w_e3_l, w_e2_l):
    shift1, scale1, gate1, shift2, scale2, gate2 = jnp.split(mod, 6, axis=-1)
    y, states = token_mixing(x * (1 + scale1) + shift1, latent, mC0, mn0, mm0, hS0, ctx_k, ctx_v,
                             w_in_l, b_in_l, fbias_l, lb_l, rpb_l, w_branch_l, w_out_l)
    x = layer_norm(DEEPNORM_ALPHA * x + gate1 * y, ln_g_l[0], ln_b_l[0])
    y = hier_moe(x * (1 + scale2) + shift2, w_rg_l, w_re_l, w_e1_l, w_e3_l, w_e2_l)
    x = layer_norm(DEEPNORM_ALPHA * x + gate2 * y, ln_g_l[1], ln_b_l[1])
    return x, states

def setup_inputs(seed: int = 0) -> dict:
    key = jax.random.key(seed)
    ks = jax.random.split(key, 32)
    D = D_MODEL

    def nrm(k, shape, s):
        return jax.random.normal(k, shape, jnp.float32) * s

    return {
        'x_prompt': nrm(ks[0], (BATCH, SEQ, D), 1.0),
        'x_sample': nrm(ks[1], (DEC_BATCH, DEC_SEQ, D), 1.0),
        'c': nrm(ks[2], (DEC_BATCH, D), 1.0),
        'cache_na_k': nrm(ks[3], (DEC_BATCH, DEPTH, NA_HEADS, PAST_LEN, NA_DH), 1.0),
        'cache_na_v': nrm(ks[4], (DEC_BATCH, DEPTH, NA_HEADS, PAST_LEN, NA_DH), 1.0),
        'state_mlstm_C': nrm(ks[5], (DEC_BATCH, DEPTH, 2, MA_HEADS, MA_DK, MA_DV), 0.1),
        'state_mlstm_n': nrm(ks[6], (DEC_BATCH, DEPTH, 2, MA_HEADS, MA_DK), 0.1),
        'state_mlstm_m': nrm(ks[7], (DEC_BATCH, DEPTH, 2, MA_HEADS), 1.0),
        'state_hgrn': nrm(ks[8], (DEC_BATCH, DEPTH, 2, HG_HEADS, HG_DK, HG_DV), 1.0),
        'c_ctx': nrm(ks[9], (D,), 1.0),
        'w_mod': nrm(ks[10], (DEPTH, D, 6 * D), 0.5 * D ** -0.5),
        'b_mod': nrm(ks[11], (DEPTH, 6 * D), 0.02),
        'w_in': nrm(ks[12], (DEPTH, D, N_IN), D ** -0.5),
        'b_in': nrm(ks[13], (DEPTH, N_IN), 0.02),
        'mlstm_fbias': jnp.linspace(3.0, 6.0, MA_HEADS)[None, None, :] + nrm(ks[14], (DEPTH, 2, MA_HEADS), 0.1),
        'hgrn_lb_logits': nrm(ks[15], (2, DEPTH, HG_W), 1.0),
        'na_rpb': nrm(ks[16], (DEPTH, NA_HEADS, 2 * NA_KR_MAX - 1, 2 * NA_KC - 1), 0.1),
        'w_branch': nrm(ks[17], (DEPTH, 3, BRANCH_W, D), DEEPNORM_BETA * BRANCH_W ** -0.5),
        'w_out': nrm(ks[18], (DEPTH, D, D), DEEPNORM_BETA * D ** -0.5),
        'ln_g': 1.0 + nrm(ks[19], (DEPTH, 2, D), 0.02),
        'ln_b': nrm(ks[20], (DEPTH, 2, D), 0.02),
        'w_rg': nrm(ks[21], (DEPTH, D, N_GROUPS), D ** -0.5),
        'w_re': nrm(ks[22], (DEPTH, D, N_EXPERTS), D ** -0.5),
        'w_e1': nrm(ks[23], (DEPTH, N_EXPERTS, D, D_EXPERT), D ** -0.5),
        'w_e3': nrm(ks[24], (DEPTH, N_EXPERTS, D, D_EXPERT), D ** -0.5),
        'w_e2': nrm(ks[25], (DEPTH, N_EXPERTS, D_EXPERT, D), DEEPNORM_BETA * D_EXPERT ** -0.5),
    }

def reference(x_prompt, x_sample, c, cache_na_k, cache_na_v, state_mlstm_C, state_mlstm_n,
              state_mlstm_m, state_hgrn, c_ctx, w_mod, b_mod, w_in, b_in, mlstm_fbias,
              hgrn_lb_logits, na_rpb, w_branch, w_out, ln_g, ln_b, w_rg, w_re, w_e1, w_e3, w_e2):
    f32 = jnp.float32
    lb_cum = jnp.cumsum(jax.nn.softmax(hgrn_lb_logits.astype(f32), axis=1), axis=1)
    lb_all = lb_cum - lb_cum[:, :1]

    xp = x_prompt
    B_ = xp.shape[0]
    zC = jnp.zeros((B_, 2, MA_HEADS, MA_DK, MA_DV), f32)
    zn = jnp.zeros((B_, 2, MA_HEADS, MA_DK), f32)
    zm = jnp.zeros((B_, 2, MA_HEADS), f32)
    zS = jnp.zeros((B_, 2, HG_HEADS, HG_DK, HG_DV), f32)
    ks_, vs_, Cs, ns, ms, Ss = [], [], [], [], [], []
    for l in range(DEPTH):
        mod = (jax.nn.silu(c_ctx) @ w_mod[l] + b_mod[l])[None, None, :]
        xp, st = trunk_layer(xp, mod, False, zC, zn, zm, zS, None, None,
                             w_in[l], b_in[l], mlstm_fbias[l], lb_all[:, l], na_rpb[l], w_branch[l], w_out[l],
                             ln_g[l], ln_b[l], w_rg[l], w_re[l], w_e1[l], w_e3[l], w_e2[l])
        ks_.append(st[0]); vs_.append(st[1]); Cs.append(st[2]); ns.append(st[3]); ms.append(st[4]); Ss.append(st[5])
    dt = x_prompt.dtype
    new_na_k = jnp.stack(ks_, 1)
    new_na_v = jnp.stack(vs_, 1)
    new_mlstm_C = jnp.stack(Cs, 1).astype(dt)
    new_mlstm_n = jnp.stack(ns, 1).astype(dt)
    new_mlstm_m = jnp.stack(ms, 1).astype(dt)
    new_hgrn = jnp.stack(Ss, 1).astype(dt)
    y_prompt = xp

    xs = x_sample
    for l in range(DEPTH):
        mod = (jax.nn.silu(c) @ w_mod[l] + b_mod[l])[:, None, :]
        xs, _ = trunk_layer(xs, mod, True, state_mlstm_C[:, l], state_mlstm_n[:, l], state_mlstm_m[:, l],
                            state_hgrn[:, l], cache_na_k[:, l], cache_na_v[:, l],
                            w_in[l], b_in[l], mlstm_fbias[l], lb_all[:, l], na_rpb[l], w_branch[l], w_out[l],
                            ln_g[l], ln_b[l], w_rg[l], w_re[l], w_e1[l], w_e3[l], w_e2[l])
    y_sample = xs
    return (y_prompt, y_sample, new_na_k, new_na_v, new_mlstm_C, new_mlstm_n, new_mlstm_m, new_hgrn)


_drawn_inputs = setup_inputs


def setup_inputs(seed=0):
    import zlib

    import numpy as np

    out = dict(_drawn_inputs(seed))
    spreads = {}
    factors = {'cache_na_k': 6.038,
     'cache_na_v': 4.441,
     'state_mlstm_C': 5.222,
     'state_mlstm_n': 2.823,
     'state_mlstm_m': 3.938,
     'state_hgrn': 120.54,
     'na_rpb': 64.0}
    for name, (base, spread) in spreads.items():
        noise = np.random.default_rng([zlib.crc32(name.encode()), seed]).standard_normal(out[name].shape)
        drawn = base * np.exp(spread * noise) if base else spread * noise
        out[name] = __import__('jax').numpy.asarray(drawn.astype(out[name].dtype))
    for name, factor in factors.items():
        out[name] = (out[name] * factor).astype(out[name].dtype)
    return out
```

```python
from contextlib import ExitStack

import numpy as np

import concourse.bass as bass
from concourse import mybir

F32 = mybir.dt.float32
U8 = mybir.dt.uint8
ALU = mybir.AluOpType
ACT = mybir.ActivationFunctionType
X = mybir.AxisListType.X

P = 128
D = 1024
DEPTH = 2
G = 2
KT = D // P
W = 512
HEADS = 4
DK = 128
NAH, NAD = 8, 64
BT = W // P
NE = 16
FE = 512
GRID_W = 64
NEG = -1.0e30
TINY = 1.0e-19
LN_EPS, RMS_EPS = 1e-5, 1e-6
ALPHA = (2 * DEPTH) ** 0.25
QSCALE = DK ** -0.5
NSCALE = NAD ** -0.5

RING = 3
SLOT = KT * W
N_MOD, N_IN, N_BR, N_OUT = 12, 18, 3, 2
FIRST_EXPERT_SLOT = N_MOD + N_IN + N_BR + N_OUT + 1
SLOTS = FIRST_EXPERT_SLOT + 3 * NE
assert FIRST_EXPERT_SLOT % RING == 0 and SLOTS % RING == 0 and N_MOD % RING == 0

CF_F, CF_B, CQ, CI, AQ, AK, AV, AO, BQ, BK, BV, CG = range(12)
CHUNK_COL = [3600, 4112, 4624, 5136, 0, 512, 1024, 1536, 2064, 2576, 3088, 5648] + [6160 + W * j for j in range(6)]
GATES_COL = 2048
GATE_BUF = [CF_F, CF_B, CQ, CI, AQ, AK]
LEVELS = [64, 32, 16, 8, 4, 2, 1]
NL = len(LEVELS)

MOD_COLS = {0: 0, 1: 4, 2: 8, 3: 12, 6: 16, 7: 20, 8: 24, 9: 28}
MOD_ROWS = {4: 0, 5: 1, 10: 2, 11: 3}
SHIFT, SCALE = (0, 16), (8, 24)



def fields(sizes):
    at, out = 0, {}
    for name, n in sizes:
        out[name] = (at, n)
        at += n
    return out, at


CONST, N_CONST = fields([("ident", P), ("ones", P), ("tri_f", P), ("tri_b", P), ("rest_f", P), ("rest_b", P),
                         ("below", P), ("above", P), ("level_f", NL * P), ("level_b", NL * P),
                         ("cos", P), ("sin", P),
                         ("level_mask", 2 * NL * P // 4)])
LDATA, N_LDATA = fields([("C0", 2 * W), ("S0", 2 * W), ("rpb", 2 * W), ("ck", W), ("cv", W), ("w_gates", KT * 16),
                         ("w_route", KT * 20), ("b_gates", 16), ("fbias", 8), ("n0", 8), ("m0", 16), ("b_mod", 32),
                         ("b_rows", W), ("past", DEPTH)])

H_ROUNDS = []
for _g in range(G):
    H_ROUNDS += [("prep", _g, 0), ("turn", _g, 0)] + [("level", _g, i) for i in range(NL + 1)] + [("out", _g, 0)]
H_ROUNDS += [("gate", 0, 0), ("gate", 1, 0)]
T_ROUNDS = [("forget", 0, 0), ("cumsum", 0, 0)]
for _g in range(G):
    T_ROUNDS += [("max", _g, 0), ("decay", _g, 0), ("turn", _g, 0), ("scores", _g, 0), ("read_f", _g, 0), ("read_b", _g, 0)]
    T_ROUNDS += [("state", 0, 0), ("norm_state", 0, 0)] if _g == 0 else [("inter_b", 1, 0)]
    T_ROUNDS += [("gate", _g, 0)]
for _g in range(G):
    T_ROUNDS += [("na_turn", _g, 0)] + [("na_cache", _g, 0)] * (_g == 1)
    for _p in range(2):
        T_ROUNDS += [("na_scores", _g, _p), ("na_probs", _g, _p), ("na_out", _g, _p)]
NH, NT = len(H_ROUNDS), len(T_ROUNDS)
QUARTERS = 4 * N_IN


def ready_quarter(chunk, g):
    return 4 * chunk + 2 * g + 2


def plan(rounds, first, needs):
    at, q = [], first
    for r in rounds:
        q = max([q] + [ready_quarter(c, g) for c, g in needs(r)])
        at.append(q)
        q += 1
    return at


def h_needs(r):
    kind, g, _ = r
    return {"prep": [(CQ, g)], "out": [(CI, g)], "gate": [(CG, g)]}.get(kind, [])


def t_needs(r):
    kind, g, _ = r
    return {"turn": [(AK, g)], "read_f": [(AV, g)], "gate": [(AO, g)], "na_turn": [(BK, g)], "na_out": [(BV, g)]}.get(kind, [])


H_AT = plan(H_ROUNDS, 0, h_needs)
T_AT = plan(T_ROUNDS, 12, t_needs)
assert max(H_AT + T_AT) < QUARTERS
assert all(ready_quarter(12 + j, 0) - 1 > (H_AT[-3] if j < 4 else T_AT[T_ROUNDS.index(("gate", 1, 0))]) for j in range(6))



def build(nc, dram, out):
    ctx = ExitStack()
    with ctx:
        def sb(name, shape, dt=F32):
            return ctx.enter_context(nc.sbuf_tensor(name, shape, dt))

        def sem(name):
            return ctx.enter_context(nc.semaphore(name))

        ring = sb("ring", [P, RING, SLOT])
        bias_ring = sb("bias_ring", [P, RING, W])
        const = sb("const", [P, N_CONST])
        ldata = sb("ldata", [P, N_LDATA])
        x = sb("x", [P, G, D])
        hT = sb("hT", [P, KT, G * P])
        ch = sb("ch", [P, G, 12, W])
        lb = sb("lb", [P, 2, W])
        scT = sb("scT", [P, KT, G])
        scZ = sb("scZ", [P, KT, 4, 8])
        mod = sb("mod", [P, 32, G])
        grow = sb("grow", [8, W])
        hbuf = sb("hbuf", [P, 13 * W])
        o_norm = sb("o_norm", [P, G, W])
        tbuf = sb("tbuf", [P, 8 * W])
        sm = sb("sm", [P, 640])

        log_f = hbuf[:, 0:2 * W].rearrange("p (d n) -> p d n", d=2)
        k_T = hbuf[:, 2 * W:4 * W].rearrange("p (d n) -> p d n", d=2)
        decay = hbuf[:, 4 * W:6 * W].rearrange("p (d n) -> p d n", d=2)
        q_dec = hbuf[:, 6 * W:8 * W].rearrange("p (d n) -> p d n", d=2)
        k_dec = hbuf[:, 8 * W:10 * W].rearrange("p (d n) -> p d n", d=2)
        q_T = hbuf[:, 10 * W:11 * W]
        att = hbuf[:, 11 * W:12 * W]
        o_sb = hbuf[:, 12 * W:13 * W]
        hsig = hbuf[:, 4 * W:7 * W]
        y = hbuf[:, 0:4 * W].rearrange("p (g n) -> p g n", g=G)
        lnb = hbuf[:, 4 * W:8 * W].rearrange("p (a n) -> p a n", a=2)
        grep = hbuf[:, 8 * W:9 * W]
        lnt = hbuf[:, 9 * W:13 * W].rearrange("p (g n) -> p g n", g=G)
        brT = tbuf[:, 0:4 * W].rearrange("p (b k t) -> p b k t", b=2, k=BT)

        em = tbuf[:, 0:2 * W].rearrange("p (d n) -> p d n", d=2)
        dg = tbuf[:, 2 * W:4 * W].rearrange("p (d n) -> p d n", d=2)
        am = tbuf[:, 4 * W:5 * W]
        qTa = tbuf[:, 5 * W:6 * W]
        kTa = tbuf[:, 6 * W:7 * W]
        hs = tbuf[:, 7 * W:8 * W]
        na_s, na_pT, na_cT, na_qT, na_kT = em, dg, am, qTa, kTa
        chf = ch[:, :, :, :].rearrange("p g c n -> p (g c n)")
        y_moe = chf[:, 0:4 * W].rearrange("p (g n) -> p g n", g=G)
        den_e = chf[:, 4 * W:6 * W].rearrange("p (g n) -> p g n", g=G)
        hid = chf[:, 6 * W:8 * W].rearrange("p (g n) -> p g n", g=G)
        hidT = chf[:, 8 * W:10 * W].rearrange("p (g n) -> p g n", g=G)
        lb_e = chf[:, 10 * W:14 * W].rearrange("p (d j n) -> p d j n", d=2, j=DEPTH)
        lb_m = chf[:, 14 * W:16 * W].rearrange("p (d n) -> p d n", d=2)

        small_at = [0]

        def small(*shape):
            n = int(np.prod(shape))
            a = small_at[0]
            small_at[0] += n
            v = sm[:, a:a + n]
            if len(shape) == 2:
                v = v.rearrange("p (a b) -> p a b", a=shape[0])
            if len(shape) == 3:
                v = v.rearrange("p (a b c) -> p a b c", a=shape[0], b=shape[1])
            return v

        ig = small(2, G, 4)
        fz = small(2, G, 4)
        fn = small(2, G, 4)
        lf = small(2, G, 4)
        bc = small(2, G, 4)
        mx = small(2, G, 4)
        mt = small(2, G, 4)
        wi = small(2, G, 4)
        ex = small(2, G, 4)
        dn = small(2, 4)
        rr = small(2, 4)
        ws = small(2, 4)
        h4 = small(4)
        h4b = small(4)
        n_mx = small(4)
        n_mb = small(4)
        n_sum = small(2, 4)
        bn6 = small(2, 6)
        bn2 = small(2)
        rstd = small(1)
        lg = small(G, 20)
        r_d = small(G, 4)
        r_mx, r_p, r_m1, r_m2, r_e, r_w = (small(G) for _ in range(6))
        r_pre = small(G)
        r_sel, r_o1, r_o2, r_le, r_eq, r_in = (small(G, 4) for _ in range(6))
        r_x = small(G, 4, 4)
        gw = small(G, NE)
        psum = ctx.enter_context(nc.psum_tensor("psum", [P, 8, W], F32))
        PJ, EX, PP, T = 0, 2, 4, 6

        def bank(b, n=1):
            return psum[:, b, :] if n == 1 else psum[:, b:b + n, :]

        def heads(ap):
            return ap.rearrange("p (h n) -> p h n", h=HEADS)

        def over_heads(ap):
            return ap.unsqueeze(1).to_broadcast([P, HEADS, P])

        def over_cols(ap, n=P):
            return ap.unsqueeze(2).to_broadcast([P, 4, n])

        def c_(name):
            a, n = CONST[name]
            return const[:, a:a + n]

        def l_(name):
            a, n = LDATA[name]
            return ldata[:, a:a + n]

        ident, ones = c_("ident"), c_("ones")
        level_mask = c_("level_mask").bitcast(U8).rearrange("p (d i n) -> p d i n", d=2, i=NL)
        tri = [c_("tri_f"), c_("tri_b")]
        rest = [c_("rest_f"), c_("rest_b")]
        mask = [c_("below"), c_("above")]
        level = [c_("level_f").rearrange("p (i n) -> p i n", i=NL), c_("level_b").rearrange("p (i n) -> p i n", i=NL)]
        C0 = l_("C0").rearrange("p (d h n) -> p d h n", d=2, h=HEADS)
        S0 = l_("S0").rearrange("p (d h n) -> p d h n", d=2, h=HEADS)
        sig = l_("b_rows")
        rpb = l_("rpb").rearrange("p (a n) -> p a n", a=2)
        w_gates = l_("w_gates").rearrange("p (k n) -> p k n", k=KT)
        w_route = l_("w_route").rearrange("p (k n) -> p k n", k=KT)
        m0 = l_("m0").rearrange("p (d g h) -> p d g h", d=2, g=G)

        start_loaded = sem("start_loaded")
        ldata_loaded = sem("ldata_loaded")
        ldata_free = sem("ldata_free")
        slot_loaded = [sem(f"slot_loaded{i}") for i in range(RING)]
        bias_loaded = [sem(f"bias_loaded{i}") for i in range(RING)]
        slot_used = sem("slot_used")
        ln_loaded = sem("ln_loaded")
        silu_c = sem("silu_c")
        exp_c = sem("exp_c")
        lb_max = sem("lb_max")
        lb_exp = sem("lb_exp")
        mod_ready = sem("mod_ready")
        x_ready = sem("x_ready")
        xt_filled = sem("xt_filled")
        xt_read = sem("xt_read")
        proj_filled = sem("proj_filled")
        proj_read = sem("proj_read")
        sig_exp = sem("sig_exp")
        sig_done = sem("sig_done")
        h_pe, h_act, h_dve, h_pool = sem("h_pe"), sem("h_act"), sem("h_dve"), sem("h_pool")
        t_pe, t_act, t_dve, t_pool = sem("t_pe"), sem("t_act"), sem("t_dve"), sem("t_pool")
        h_scores = sem("h_scores")
        h_exp = sem("h_exp")
        h_sigmoid = sem("h_sigmoid")
        h_forget = sem("h_forget")
        h_square = sem("h_square")
        t_half = sem("t_half")
        t_back = sem("t_back")
        br_turned = sem("br_turned")
        br_ready = sem("br_ready")
        br_filled = sem("br_filled")
        br_added = sem("br_added")
        yt_filled = sem("yt_filled")
        yt_ready = sem("yt_ready")
        out_filled = sem("out_filled")
        out_added = sem("out_added")
        grep_filled = sem("grep_filled")
        grep_ready = sem("grep_ready")
        ln_var = sem("ln_var")
        ln_rstd = sem("ln_rstd")
        rt_filled = sem("rt_filled")
        rt_half = sem("rt_half")
        rt_exp = sem("rt_exp")
        gate_ready = sem("gate_ready")
        up_filled = sem("up_filled")
        up_exp = sem("up_exp")
        hid_ready = sem("hid_ready")
        hid_turned = sem("hid_turned")
        hidT_ready = sem("hidT_ready")
        down_filled = sem("down_filled")
        down_added = sem("down_added")
        dve_chain, pool_chain, act_chain = sem("dve_chain"), sem("pool_chain"), sem("act_chain")
        moe_chain = sem("moe_chain")
        dve_tick, pool_tick = sem("dve_tick"), sem("pool_tick")
        kv_stored = sem("kv_stored")
        state_stored = sem("state_stored")
        hgrn_stored = sem("hgrn_stored")
        y_stored = sem("y_stored")
        N_STATE = 4 * 16

        class Chain:

            def __init__(self, eng, s, per, index=0):
                self.eng, self.s, self.per, self.index, self.n = eng, s, per, index, 0

            def __call__(self, ins, alone=None):
                self.n += 1
                ins.then_inc(self.s, 1)
                self.eng.wait_ge(self.s, self.index * self.per + self.n)
                if alone is not None:
                    self.eng.sem_inc(alone, 1)

            def close(self):
                assert self.n <= self.per, (self.s, self.n)
                if self.n < self.per:
                    self.eng.sem_inc(self.s, self.per - self.n)

        def proj(l, c, g):
            return l * (2 * N_IN) + (2 * RING + 2 * c + g + 1)

        def used(l, i):
            return l * SLOTS + (RING + i + 1)

        def arrived(l, i):
            return l * (SLOTS // RING * 16) + (i // RING + 1) * 16

        N_HALF = {"forget": 2, "decay": 1, "na_scores": 1}
        half_before = [sum(N_HALF.get(r[0], 0) for r in T_ROUNDS[:n]) for n in range(NT)]
        halves = sum(N_HALF.get(r[0], 0) for r in T_ROUNDS)

        def half(l, n, i=0):
            return l * halves + (half_before[n] + i + 1)

        def in_order(h_round, t_round, q):
            for n in range(NH):
                if H_AT[n] == q:
                    h_round(n)
            for n in range(NT):
                if T_AT[n] == q:
                    t_round(n)

        T_CHUNK = {(kind, g): c for g in range(G) for kind, c in (("turn", AK), ("read_f", AV), ("na_turn", BK), ("na_out", BV))}

        block = ctx.enter_context(nc.Block())

        @block.sync
        def _(sp):
            for dst, src in ((const[:, :], dram["const"]), (x[:, :, :], dram["x"]), (scT[:, :, :], dram["c_cols"])):
                sp.dma_start(dst, src).then_inc(start_loaded, 16)

            def load(l, i, j):
                sp.wait_ge(slot_used, l * SLOTS + (i + 1))
                sp.dma_start(ring[:, j, :], dram["stream"][l * SLOTS + i]).then_inc(slot_loaded[j], 16)

            with sp.Fori(0, DEPTH) as l:
                sp.wait_ge(ldata_free, l + 1)
                sp.dma_start(lb_e, dram["lb_logits"]).then_inc(ldata_loaded, 16)
                sp.dma_start(ldata[:, :], dram["ldata"][l]).then_inc(ldata_loaded, 16)
                for i in range(N_MOD):
                    load(l, i, i % RING)
                for c in range(N_IN):
                    load(l, N_MOD + c, c % RING)
                    sp.wait_ge(proj_read, l * (2 * N_IN) + (2 * c + 2))
                    sp.dma_start(bias_ring[:, c % RING, :], dram["b_in"][l * N_IN + c]).then_inc(bias_loaded[c % RING], 16)
                for i in range(N_MOD + N_IN, FIRST_EXPERT_SLOT):
                    load(l, i, i % RING)
                    if i == N_MOD + N_IN:
                        sp.wait_ge(h_dve, l * NH + NH)
                        sp.wait_ge(h_act, l * NH + NH)
                        sp.wait_ge(h_pool, l * NH + NH)
                        sp.wait_ge(state_stored, l * N_STATE + N_STATE)
                        sp.dma_start(lnb, dram["ln"][l * 2]).then_inc(ln_loaded, 16)
                sp.wait_ge(x_ready, l * 2 + 2)
                sp.dma_start(lnb, dram["ln"][l * 2 + 1]).then_inc(ln_loaded, 16)
                with sp.Fori(0, NE) as e:
                    for j in range(3):
                        sp.wait_ge(slot_used, l * SLOTS + e * 3 + (FIRST_EXPERT_SLOT + j + 1))
                        sp.dma_start(ring[:, j, :], dram["stream"][l * SLOTS + e * 3 + (FIRST_EXPERT_SLOT + j)])\
                          .then_inc(slot_loaded[j], 16)
            sp.wait_ge(x_ready, 2 * DEPTH + 1)
            for g in range(G):
                sp.dma_start(out["y"][g], x[:, g, :]).then_inc(y_stored, 16)
            sp.wait_ge(y_stored, 16 * G)
            sp.wait_ge(kv_stored, 32 * DEPTH)
            sp.wait_ge(state_stored, N_STATE * DEPTH)
            sp.wait_ge(hgrn_stored, 16 * DEPTH)

        @block.tensor
        def _(pe):
            pe.sem_inc(slot_used, RING)
            pe.sem_inc(down_filled, 4)
            pe.sem_inc(hid_turned, 2)
            pe.wait_ge(start_loaded, 48)
            pe.wait_ge(silu_c, 1)

            def slot(l, i):
                pe.wait_ge(slot_loaded[i % RING], arrived(l, i))
                return ring[:, i % RING, :].rearrange("p (k n) -> p k n", k=KT)

            def turn(b, src):
                for j in range(4):
                    mm = pe.transpose(psum[:, b, j * P:(j + 1) * P], src[:, j * P:(j + 1) * P], ident)
                return mm

            def turn_x(l, sub):
                pe.wait_ge(x_ready, l * 2 + (sub + 1))
                for g in range(G):
                    for b in range(2):
                        turn(2 * g + b, x[:, g, b * W:(b + 1) * W]).then_inc(xt_filled, 1)
                pe.wait_ge(xt_read, l * 8 + (4 * sub + 4))

            def gate_row(l, sub, half_, g):
                n = 4 * sub + 2 * half_ + g
                if n in (0, 1):
                    pe.wait_ge(yt_ready, l * 4 + 4)
                elif n in (4, 5):
                    pe.wait_ge(hidT_ready, l * (2 * NE) + 2 * NE)
                else:
                    pe.wait_ge(grep_ready, l * 8 + (n - 1))
                pe.matmul(bank(4 + n % 2), ident[0:8, n:n + 1].to_broadcast([8, P]), grow[:, :], start=True, stop=True).then_inc(grep_filled, 1)

            with pe.Fori(0, DEPTH) as l:
                pe.wait_ge(ldata_loaded, l * 32 + 32)

                def h_round(n):
                    kind, g, i = H_ROUNDS[n]
                    if n:
                        pe.wait_ge(h_act, l * NH + n)
                        pe.wait_ge(h_dve, l * NH + n)
                        pe.wait_ge(h_pool, l * NH + n)
                    if kind in ("prep", "gate"):
                        pe.sem_inc(h_pe, 1)
                    if kind == "turn":
                        turn(EX, ch[:, g, CQ, :])
                        turn(EX + 1, ch[:, g, CF_F, :])
                        turn(PP, ch[:, g, CF_B, :]).then_inc(h_pe, 1)
                    if kind == "level":
                        for d in range(2 if i else 1):
                            for h in range(HEADS):
                                hp = slice(h * P, (h + 1) * P)
                                mm = pe.matmul(psum[:, PP + d, hp], k_dec[:, d, hp], q_dec[:, d, hp] if i else q_T[:, hp],
                                               start=True, stop=True)
                        mm.then_inc(h_scores, 1)
                        for d in range(2):
                            if i == NL and g == 0:
                                mm = pe.matmul(bank(EX + d), rest[d], log_f[:, d, :], start=True, stop=True)
                                continue
                            for h in range(HEADS):
                                mm = pe.matmul(psum[:, EX + d, h * P:(h + 1) * P], log_f[:, d, h * P:(h + 1) * P],
                                               level[d][:, i, :] if i < NL else tri[d], start=True, stop=True)
                        mm.then_inc(h_pe, 1)
                    if kind == "out":
                        pe.wait_ge(proj_read, proj(l, CI, g))
                        if g == 0:
                            for d in range(2):
                                for h in range(HEADS):
                                    hp = slice(h * P, (h + 1) * P)
                                    pe.matmul(psum[:, EX + d, hp], k_dec[:, d, hp], ch[:, g, CI, hp], start=True, stop=True)
                        for h in range(HEADS):
                            hp = slice(h * P, (h + 1) * P)
                            mm = pe.matmul(psum[:, PP, hp], att[:, hp], ch[:, g, CI, hp], start=True, stop=(g == 0))
                            if g == 1:
                                for d in range(2):
                                    mm = pe.matmul(psum[:, PP, hp], q_dec[:, d, hp], S0[:, d, h, :], start=False, stop=(d == 1))
                        mm.then_inc(h_pe, 1)

                def t_round(n):
                    kind, g, i = T_ROUNDS[n]
                    if n:
                        pe.wait_ge(t_act, l * NT + n)
                        pe.wait_ge(t_dve, l * NT + n)
                        pe.wait_ge(t_pool, l * NT + n)
                    if (kind, g) in T_CHUNK:
                        pe.wait_ge(proj_read, proj(l, T_CHUNK[kind, g], g))
                    mm = None
                    tiles = [slice(h * P, (h + 1) * P) for h in range(HEADS)]
                    if kind == "forget":
                        for gg in range(G):
                            for k in range(KT):
                                mm = pe.matmul(psum[:, T, gg * 16:gg * 16 + 16], hT[:, k, gg * P:(gg + 1) * P], w_gates[:, k, :],
                                               start=(k == 0), stop=(k == KT - 1))
                    if kind == "cumsum":
                        for d in range(2):
                            mm = pe.matmul(psum[:, T, d * 8:d * 8 + 8], tri[d], lf[:, d, :, :].rearrange("p g h -> p (g h)"),
                                           start=True, stop=True)
                    if kind in ("max", "decay"):
                        for d in range(2):
                            mm = pe.matmul(bank(T + d), ones, dg[:, d, :], start=True, stop=True)
                    if kind == "turn":
                        turn(T, ch[:, g, AQ, :])
                        mm = turn(T + 1, ch[:, g, AK, :])
                    if kind == "scores":
                        for hp in tiles:
                            mm = pe.matmul(psum[:, T, hp], kTa[:, hp], qTa[:, hp], start=True, stop=True)
                    if kind == "read_f":
                        for j in range(8):
                            pe.matmul(psum[:, T + 1, j:j + 1], em[:, j // 4, tiles[j % 4]], ones[:, 0:1], start=True, stop=True)
                            if g == 1:
                                pe.matmul(psum[:, T + 1, 8 + j:9 + j], qTa[:, tiles[j % 4]], l_("n0")[:, j:j + 1], start=True, stop=True)
                        for hp in tiles:
                            mm = pe.matmul(psum[:, T, hp], em[:, 0, hp], ch[:, g, AV, hp], start=True, stop=True)
                    if kind == "read_b":
                        for h, hp in enumerate(tiles):
                            mm = pe.matmul(psum[:, T, hp], em[:, 1, hp], ch[:, g, AV, hp], start=True, stop=True)
                        if g == 1:
                            for h, hp in enumerate(tiles):
                                mm = pe.matmul(psum[:, T + 1, hp], qTa[:, hp], C0[:, 0, h, :], start=True, stop=True)
                    if kind == "inter_b":
                        for h, hp in enumerate(tiles):
                            mm = pe.matmul(psum[:, T, hp], qTa[:, hp], C0[:, 1, h, :], start=True, stop=True)
                    if kind == "state":
                        for d in range(2):
                            for hp in tiles:
                                mm = pe.matmul(psum[:, T + d, hp], dg[:, d, hp], ch[:, 0, AV, hp], start=True, stop=True)
                    if kind == "norm_state":
                        for d in range(2):
                            mm = pe.matmul(psum[0:1, T + d, :], ones[:, 0:1], dg[:, d, :], start=True, stop=True)
                    if kind == "na_turn":
                        turn(T, ch[:, g, BQ, :])
                        mm = turn(T + 1, ch[:, g, BK, :])
                    if kind == "na_cache":
                        mm = turn(T, l_("ck"))
                    if kind == "na_scores":
                        o = NAD * i
                        for jp in tiles:
                            mm = pe.matmul(psum[:, T, jp], na_qT[o:o + NAD, jp], na_kT[o:o + NAD, jp], start=True, stop=True)
                        if g == 1:
                            for jp in tiles:
                                mm = pe.matmul(psum[:, T + 1, jp], na_qT[o:o + NAD, jp], na_cT[o:o + NAD, jp], start=True, stop=True)
                    if kind == "na_probs":
                        mm = turn(T, na_s[:, 0, :])
                        if g == 1:
                            mm = turn(T + 1, na_s[:, 1, :])
                    if kind == "na_out":
                        for j, jp in enumerate(tiles):
                            hc = slice((2 * j + i) * NAD, (2 * j + i + 1) * NAD)
                            o = psum[:, T, j * NAD:(j + 1) * NAD]
                            mm = pe.matmul(o, na_pT[:, 0, jp], ch[:, g, BV, hc], start=True, stop=(g == 0))
                            if g == 1:
                                mm = pe.matmul(o, na_pT[:, 1, jp], l_("cv")[:, hc], start=False, stop=True)
                    if mm is None:
                        pe.sem_inc(t_pe, 1)
                    else:
                        mm.then_inc(t_pe, 1)

                n = 0
                for c in range(N_MOD):
                    w = slot(l, c)
                    if c in MOD_COLS:
                        for j in range(4):
                            o = psum[:, T, (MOD_COLS[c] + j) * G:(MOD_COLS[c] + j + 1) * G]
                            for k in range(KT):
                                mm = pe.matmul(o, w[:, k, j * P:(j + 1) * P], scT[:, k, :], start=(k == 0), stop=(k == KT - 1))
                    else:
                        for k in range(KT):
                            mm = pe.matmul(psum[0:8, T + 1, :], scZ[:, k, MOD_ROWS[c], :], w[:, k, :],
                                           start=(n == 0), stop=(n == 4 * KT - 1))
                            n += 1
                    mm.then_inc(slot_used, 1)
                turn_x(l, 0)
                for q in range(QUARTERS):
                    in_order(h_round, t_round, q)
                    c, g, part = q // 4, (q // 2) % 2, q % 2
                    w = slot(l, N_MOD + c)
                    if part == 0 and c:
                        pe.wait_ge(proj_read, proj(l, c - 1, g))
                    for k in range(4 * part, 4 * part + 4):
                        mm = pe.matmul(bank(PJ + g), hT[:, k, g * P:(g + 1) * P], w[:, k, :], start=(k == 0), stop=(k == KT - 1))
                    if part:
                        mm.then_inc(slot_used if g else proj_filled, 1)
                pe.wait_ge(h_dve, l * NH + NH)
                pe.wait_ge(t_dve, l * NT + NT)
                pe.wait_ge(proj_read, proj(l, N_IN - 1, 1))
                for b, src in enumerate((AO, BQ, CG)):
                    if b:
                        pe.wait_ge(br_ready, l * 3 + b)
                    for g in range(G):
                        for k in range(BT):
                            mm = pe.transpose(psum[:, T + k // 2, (k % 2) * 256 + g * P:(k % 2) * 256 + (g + 1) * P],
                                              ch[:, g, src, k * P:(k + 1) * P], ident)
                    mm.then_inc(br_turned, 1)
                    w = ring[:, (N_MOD + N_IN + b) % RING, :].rearrange("p (k n) -> p k n", k=BT)
                    slot(l, N_MOD + N_IN + b)
                    pe.wait_ge(br_ready, l * 3 + (b + 1))
                    for g in range(G):
                        for hf in range(2):
                            if b:
                                pe.wait_ge(br_added, l * 12 + (4 * (b - 1) + 2 * g + hf + 1))
                            for k in range(BT):
                                mm = pe.matmul(bank(2 * g + hf), brT[:, b % 2, k, g * P:(g + 1) * P],
                                               w[:, k, hf * W:(hf + 1) * W], start=(k == 0), stop=(k == BT - 1))
                            mm.then_inc(slot_used if (g, hf) == (1, 1) else br_filled, 1)
                for g in range(G):
                    for b in range(2):
                        pe.wait_ge(br_added, l * 12 + (8 + 2 * g + b + 1))
                        turn(4 + 2 * g + b, y[:, g, b * W:(b + 1) * W]).then_inc(yt_filled, 1)
                pe.wait_ge(yt_ready, l * 4 + 4)
                for hf in range(2):
                    w = slot(l, N_MOD + N_IN + N_BR + hf)
                    for g in range(G):
                        gate_row(l, 0, hf, g)
                        if (hf, g) == (1, 1):
                            slot(l, FIRST_EXPERT_SLOT - 1)
                        for k in range(KT):
                            mm = pe.matmul(bank(2 * hf + g), hT[:, k, g * P:(g + 1) * P], w[:, k, :],
                                           start=(k == 0), stop=(k == KT - 1))
                        mm.then_inc(slot_used if g else out_filled, 1 + hf * g)
                turn_x(l, 1)
                for g in range(G):
                    for k in range(KT):
                        mm = pe.matmul(psum[:, T, g * 20:g * 20 + 20], hT[:, k, g * P:(g + 1) * P], w_route[:, k, :],
                                       start=(k == 0), stop=(k == KT - 1))
                mm.then_inc(rt_filled, 1)
                with pe.Fori(0, NE) as e:
                    i = l * NE + e
                    for g in range(G):
                        pe.wait_ge(hid_ready, i * 2 + (g + 1))
                        for j in range(2):
                            pe.wait_ge(slot_loaded[j], l * (SLOTS // RING * 16) + e * 16 + (FIRST_EXPERT_SLOT // RING + 1) * 16)
                            w = ring[:, j, :].rearrange("p (k n) -> p k n", k=KT)
                            for k in range(KT):
                                mm = pe.matmul(bank(2 * g + j), hT[:, k, g * P:(g + 1) * P], w[:, k, :],
                                               start=(k == 0), stop=(k == KT - 1))
                            if g:
                                mm.then_inc(slot_used, 1)
                        if not g:
                            mm.then_inc(up_filled, 1)
                    pe.wait_ge(gate_ready, l + 1)
                    pe.wait_ge(slot_loaded[2], l * (SLOTS // RING * 16) + e * 16 + (FIRST_EXPERT_SLOT // RING + 1) * 16)
                    w = ring[:, 2, :].rearrange("p (k n) -> p k n", k=BT)
                    for g in range(G):
                        pe.wait_ge(hid_ready, i * 2 + (g + 3))
                        turn(4 + g, hid[:, g, :]).then_inc(hid_turned, 1)
                        pe.wait_ge(hidT_ready, i * 2 + (g + 1))
                        for hf in range(2):
                            pe.wait_ge(down_added, i * 4 + (2 * g + hf + 1))
                            for k in range(BT):
                                mm = pe.matmul(bank(6 + hf), hidT[:, g, k * P:(k + 1) * P], w[:, k, hf * W:(hf + 1) * W],
                                               start=(k == 0), stop=(k == BT - 1))
                            if (g, hf) == (1, 1):
                                mm.then_inc(slot_used, 1)
                            else:
                                mm.then_inc(down_filled, 1)
                for hf in range(2):
                    for g in range(G):
                        gate_row(l, 1, hf, g)
                pe.wait_ge(down_added, l * (4 * NE) + (4 * NE + 2))

        @block.scalar
        def _(act):
            act.wait_ge(start_loaded, 48)
            act.activation(mod[:, 0:KT, :], scT[:, :, :], ACT.Exp, scale=-1.0).then_inc(exp_c, 1)

            with act.Fori(0, DEPTH) as l:
                link = Chain(act, act_chain, 16, l)
                act.wait_ge(lb_max, l + 1)
                act.activation(lb_e, lb_e, ACT.Exp).then_inc(lb_exp, 1)

                def h_round(n):
                    kind, g, i = H_ROUNDS[n]
                    act.wait_ge(h_pe, l * NH + (n + 1))
                    if kind == "prep":
                        act.wait_ge(proj_read, proj(l, CQ, g))
                        act.activation(hsig, ch[:, g, CF_F:CQ + 1, :].rearrange("p c n -> p (c n)"), ACT.Exp, scale=-1.0)\
                           .then_inc(h_exp, 1)
                        act.wait_ge(h_forget, l * G + (g + 1))
                        act.activation(log_f.rearrange("p d n -> p (d n)"), hsig[:, 0:2 * W], ACT.Ln).then_inc(h_act, 1)
                    elif kind == "turn":
                        act.activation(k_T[:, 0, :], bank(EX + 1), ACT.Copy)
                        act.activation(k_T[:, 1, :], bank(PP), ACT.Copy).then_inc(h_act, 1)
                    elif kind == "level":
                        act.activation(decay, bank(EX, 2), ACT.Exp).then_inc(h_act, 1)
                    elif kind == "out":
                        if g == 0:
                            link(act.activation(decay, bank(EX, 2), ACT.Copy))
                            act.dma_start(out["hgrn"][l].rearrange("d h k e -> k d h e"),
                                          decay.rearrange("p d (h n) -> p d h n", h=HEADS)).then_inc(hgrn_stored, 16)
                        act.wait_ge(h_square, l * G + (g + 1))
                        link(act.activation(h4b, h4, ACT.Ln))
                        if g == 0:
                            act.wait_ge(hgrn_stored, l * 16 + 16)
                        act.activation(h4b, h4b, ACT.Exp, scale=-0.5).then_inc(h_act, 1)
                    elif kind == "gate":
                        act.wait_ge(proj_read, proj(l, CG, g))
                        act.activation(hbuf[:, 0:W], ch[:, g, CG, :], ACT.Exp, scale=-1.0).then_inc(h_act, 1)

                def t_round(n):
                    kind, g, i = T_ROUNDS[n]
                    act.wait_ge(t_pe, l * NT + (n + 1))
                    if kind == "forget":
                        act.wait_ge(t_half, half(l, n, 0))
                        act.activation(fn, fn, ACT.Exp).then_inc(t_back, 1)
                        act.wait_ge(t_half, half(l, n, 1))
                        act.activation(fn, fn, ACT.Ln).then_inc(t_act, 1)
                    elif kind == "decay":
                        act.wait_ge(t_half, half(l, n))
                        act.wait_ge(t_pool, l * NT + n)
                        for d in range(2):
                            for h in range(HEADS):
                                hp = slice(h * P, (h + 1) * P)
                                act.activation(em[:, d, hp], em[:, d, hp], ACT.Exp, bias=ig[:, d, g, h:h + 1])
                        act.activation(wi[:, :, g, :], wi[:, :, g, :], ACT.Exp)
                        if g == 0:
                            act.activation(ws, ws, ACT.Exp)
                        act.activation(ex[:, :, g, :], mt[:, :, g, :], ACT.Exp, scale=-1.0).then_inc(t_act, 1)
                    elif kind == "turn":
                        act.activation(kTa, bank(T + 1), ACT.Copy, scale=QSCALE).then_inc(t_act, 1)
                    elif kind == "state":
                        link(act.activation(em, bank(T, 2), ACT.Copy))
                        act.dma_start(out["C"][l].rearrange("d h k e -> k d h e"),
                                      em.rearrange("p d (h n) -> p d h n", h=HEADS)).then_inc(state_stored, 16)
                        act.sem_inc(t_act, 1)
                    elif kind == "norm_state":
                        row = tbuf[0:1, 4 * W:6 * W]
                        link(act.activation(row.rearrange("p (b n) -> p b n", b=2), psum[0:1, T:T + 2, :], ACT.Copy))
                        act.dma_start(out["n"][l], row).then_inc(state_stored, 16)
                        act.dma_start(out["m"][l, 0:1, :], mt[P - 1:P, 0, 0, :]).then_inc(state_stored, 16)
                        act.dma_start(out["m"][l, 1:2, :], mt[0:1, 1, 0, :]).then_inc(state_stored, 16)
                        act.wait_ge(state_stored, l * N_STATE + N_STATE)
                        act.sem_inc(t_act, 1)
                    elif kind == "gate":
                        act.wait_ge(proj_read, proj(l, AO, g))
                        act.activation(am, ch[:, g, AO, :], ACT.Exp, scale=-1.0).then_inc(t_act, 1)
                    elif kind == "na_turn":
                        act.activation(na_qT, bank(T), ACT.Copy, scale=NSCALE).then_inc(t_act, 1)
                    elif kind == "na_scores":
                        act.wait_ge(t_half, half(l, n))
                        act.activation(tbuf[:, 0:(1 + g) * W], tbuf[:, 0:(1 + g) * W], ACT.Exp).then_inc(t_act, 1)
                    elif kind == "na_probs" and g == 1:
                        act.activation(na_pT[:, 1, :], bank(T + 1), ACT.Copy).then_inc(t_act, 1)
                    else:
                        act.sem_inc(t_act, 1)

                for q in range(QUARTERS):
                    in_order(h_round, t_round, q)
                    c, g = q // 4, (q // 2) % 2
                    if q in (4 * BK + 3, 4 * BV + 3):
                        which = "na_k" if c == BK else "na_v"
                        act.wait_ge(proj_read, proj(l, c, 0))
                        act.dma_start(out[which][l].rearrange("h t n -> t h n"),
                                      ch[:, 0, c, :].rearrange("p (h n) -> p h n", h=NAH)).then_inc(kv_stored, 16)
                    if q % 2 and c >= 12:
                        act.wait_ge(proj_read, proj(l, c, g))
                        act.wait_ge(sig_done, l * 12 + ((c - 12) * 2 + g + 1))
                        act.activation(sig, ch[:, g, GATE_BUF[c - 12], :], ACT.Exp, scale=-1.0).then_inc(sig_exp, 1)
                act.wait_ge(kv_stored, l * 32 + 32)
                for b in range(3):
                    act.wait_ge(br_turned, l * 3 + (b + 1))
                    if b == 2:
                        act.wait_ge(slot_used, used(l, N_MOD + N_IN))
                    act.activation(tbuf[:, (b % 2) * 1024:(b % 2) * 1024 + 1024].rearrange("p (b n) -> p b n", b=2),
                                   bank(T, 2), ACT.Copy).then_inc(br_ready, 1)
                for g in range(G):
                    for b in range(2):
                        act.wait_ge(yt_filled, l * 4 + (2 * g + b + 1))
                        act.activation(hT[:, 4 * b:4 * b + 4, g * P:(g + 1) * P],
                                       bank(4 + 2 * g + b).rearrange("p (k n) -> p k n", k=4), ACT.Copy).then_inc(yt_ready, 1)

                def finish(sub):
                    for n in range(4 * sub, 4 * sub + 4):
                        act.wait_ge(grep_filled, l * 8 + (n + 1))
                        act.wait_ge(out_added, l * 8 + (n + 1))
                        act.activation(grep, bank(4 + n % 2), ACT.Copy).then_inc(grep_ready, 1)
                    for g in range(G):
                        act.wait_ge(ln_var, l * 4 + (2 * sub + g + 1))
                        link(act.activation(rstd, rstd, ACT.Ln))
                        act.activation(rstd, rstd, ACT.Exp, scale=-0.5).then_inc(ln_rstd, 1)

                finish(0)
                for i, v in enumerate((r_d, r_e)):
                    act.wait_ge(rt_half, l * 2 + (i + 1))
                    act.activation(v, v, ACT.Exp).then_inc(rt_exp, 1)
                with act.Fori(0, NE) as e:
                    i = l * NE + e
                    for g in range(G):
                        if g:
                            act.wait_ge(slot_used, l * SLOTS + e * 3 + (RING + FIRST_EXPERT_SLOT + 2))
                        else:
                            act.wait_ge(up_filled, i + 1)
                        act.wait_ge(hid_ready, i * 2 + (g + 1))
                        act.activation(den_e[:, g, :], bank(2 * g), ACT.Exp, scale=-1.0).then_inc(up_exp, 1)
                    for g in range(G):
                        act.wait_ge(hid_turned, i * 2 + (g + 3))
                        act.activation(hidT[:, g, :], bank(4 + g), ACT.Copy).then_inc(hidT_ready, 1)
                finish(1)
                link.close()

        @block.vector
        def _(dve):
            tt, ts, stt = dve.tensor_tensor, dve.tensor_scalar, dve.scalar_tensor_tensor
            dve.sem_inc(ldata_free, 1)
            dve.sem_inc(x_ready, 1)
            dve.sem_inc(proj_read, 2 * RING)
            dve.sem_inc(sig_done, 1)
            dve.sem_inc(out_added, 1)
            dve.sem_inc(hid_ready, 2)
            dve.sem_inc(down_added, 2)
            dve.wait_ge(start_loaded, 48)
            dve.memset(scZ[:, :, :, :], 0.0).then_inc(dve_tick, 1)
            dve.wait_ge(exp_c, 1)
            ts(mod[:, 0:KT, :], mod[:, 0:KT, :], 1.0, None, ALU.add).then_inc(dve_tick, 1)
            dve.wait_ge(dve_tick, 2)
            dve.reciprocal(mod[:, 0:KT, :], mod[:, 0:KT, :]).then_inc(dve_tick, 1)
            dve.wait_ge(dve_tick, 3)
            tt(scT[:, :, :], scT[:, :, :], mod[:, 0:KT, :], ALU.mult).then_inc(dve_tick, 1)
            dve.wait_ge(dve_tick, 4)
            for j in range(4):
                ins = dve.tensor_copy(scZ[:, :, j, 2 * j:2 * j + 2], scT[:, :, :])
            ins.then_inc(silu_c, 1)

            with dve.Fori(0, DEPTH) as l:
                link = Chain(dve, dve_chain, 300, l)
                dve.wait_ge(ldata_loaded, l * 32 + 32)
                if DEPTH == 2:
                    link(tt(lb_m, lb_e[:, :, 0, :], lb_e[:, :, 1, :], ALU.max))
                for j in range(DEPTH):
                    ins = tt(lb_e[:, :, j, :], lb_e[:, :, j, :], lb_m, ALU.subtract)
                ins.then_inc(lb_max, 1)
                dve.wait_ge(lb_exp, l + 1)
                link(tt(lb_m, lb_e[:, :, 0, :], lb_e[:, :, 1, :], ALU.add))
                link(dve.reciprocal(lb_m, lb_m))
                link(tt(lb_m, lb_m, lb_e[:, :, 1, :], ALU.mult))
                link(ts(lb[:, :, :], lb_m, l_("past")[:, 1:2], None, ALU.mult))
                dve.wait_ge(slot_used, used(l, N_MOD - 1))
                link(tt(mod[:, :, :], psum[:, T, 0:64].rearrange("p (n g) -> p n g", g=G),
                        l_("b_mod").unsqueeze(2).to_broadcast([P, 32, G]), ALU.add))
                link(ts(mod[:, 8:16, :], mod[:, 8:16, :], 1.0, None, ALU.add))
                link(ts(mod[:, 24:32, :], mod[:, 24:32, :], 1.0, None, ALU.add))
                link(tt(grow[:, :], psum[0:8, T + 1, :], l_("b_rows")[0:8, :], ALU.add))

                def modulate(sub):
                    for n in range(4):
                        dve.wait_ge(xt_filled, l * 8 + (4 * sub + n + 1))
                        g, b = n // 2, n % 2
                        for j in range(4):
                            k = 4 * b + j
                            ins = ts(hT[:, k, g * P:(g + 1) * P], psum[:, n, j * P:(j + 1) * P],
                                     mod[:, SCALE[sub] + k, g:g + 1], mod[:, SHIFT[sub] + k, g:g + 1], ALU.mult, ALU.add)
                        ins.then_inc(xt_read, 1)

                modulate(0)

                def h_round(n):
                    kind, g, i = H_ROUNDS[n]
                    dve.wait_ge(h_pe, l * NH + (n + 1))
                    if kind == "prep":
                        dve.wait_ge(h_exp, l * G + (g + 1))
                        link(ts(hsig, hsig, 1.0, None, ALU.add))
                        dve.reciprocal(hsig, hsig).then_inc(h_sigmoid, 1)
                        dve.wait_ge(h_sigmoid, l * G + (g + 1))
                        tt(ch[:, g, CQ, :], ch[:, g, CQ, :], hsig[:, 2 * W:3 * W], ALU.mult).then_inc(h_dve, 1)
                    elif kind == "turn":
                        dve.tensor_copy(q_T, bank(EX)).then_inc(h_dve, 1)
                    elif kind == "level":
                        dve.wait_ge(h_scores, l * (G * (NL + 1)) + (g * (NL + 1) + i + 1))
                        if i == 0:
                            link(tt(heads(att), heads(bank(PP)), over_heads(ident), ALU.mult))
                        else:
                            for d in range(2):
                                dve.sem_inc(dve_tick, 1)
                                link(dve.copy_predicated(heads(att), over_heads(level_mask[:, d, i - 1, :]), heads(bank(PP + d))))
                        dve.wait_ge(h_act, l * NH + (n + 1))
                        if i < NL or g == 1:
                            tt(q_dec, decay, q_T.unsqueeze(1).to_broadcast([P, 2, W]), ALU.mult).then_inc(h_dve, 1)
                        else:
                            dve.sem_inc(h_dve, 1)
                    elif kind == "out":
                        link(dve.tensor_copy(o_sb, bank(PP)))
                        link(tt(att, o_sb, o_sb, ALU.mult))
                        link(dve.tensor_reduce(h4, heads(att), X, ALU.add))
                        ts(h4, h4, 1.0 / DK, RMS_EPS, ALU.mult, ALU.add).then_inc(h_square, 1)
                        dve.wait_ge(h_act, l * NH + (n + 1))
                        tt(heads(o_norm[:, g, :]), heads(o_sb), over_cols(h4b), ALU.mult).then_inc(h_dve, 1)
                    elif kind == "gate":
                        s = hbuf[:, 0:W]
                        dve.wait_ge(h_act, l * NH + (n + 1))
                        link(ts(s, s, 1.0, None, ALU.add))
                        link(dve.reciprocal(s, s))
                        link(tt(s, s, ch[:, g, CG, :], ALU.mult))
                        tt(ch[:, g, CG, :], s, o_norm[:, g, :], ALU.mult).then_inc(h_dve, 1)

                def t_round(n):
                    kind, g, i = T_ROUNDS[n]
                    dve.wait_ge(t_pe, l * NT + (n + 1))
                    if kind == "forget":
                        z = psum[:, T, 0:32].rearrange("p (g d t h) -> p d g t h", g=G, d=2, t=2)
                        b = l_("b_gates").rearrange("p (d t h) -> p d t h", d=2, t=2)
                        fb = l_("fbias").rearrange("p (d h) -> p d h", d=2)
                        for d in range(2):
                            tt(ig[:, d, :, :], z[:, d, :, 0, :], b[:, d, 0, :].unsqueeze(1).to_broadcast([P, G, 4]), ALU.add)
                            link(tt(fz[:, d, :, :], z[:, d, :, 1, :], b[:, d, 1, :].unsqueeze(1).to_broadcast([P, G, 4]), ALU.add))
                            link(tt(fz[:, d, :, :], fz[:, d, :, :], fb[:, d, :].unsqueeze(1).to_broadcast([P, G, 4]), ALU.add))
                        link(ts(fn, fz, -1.0, None, ALU.mult))
                        tt(fn, fn, fz, ALU.min).then_inc(t_half, 1)
                        dve.wait_ge(t_back, l + 1)
                        ts(fn, fn, 1.0, None, ALU.add).then_inc(t_half, 1)
                        link(ts(fz, fz, 0.0, None, ALU.min))
                        dve.wait_ge(t_act, l * NT + (n + 1))
                        tt(lf, fz, fn, ALU.subtract).then_inc(t_dve, 1)
                    elif kind == "cumsum":
                        flat = [v.rearrange("p d g h -> p (d g h)") for v in (bc, ig)]
                        link(dve.tensor_copy(flat[0], psum[:, T, 0:16]))
                        tt(flat[1], flat[1], flat[0], ALU.subtract).then_inc(t_dve, 1)
                    elif kind == "max":
                        for d in range(2):
                            link(tt(heads(am), heads(bank(T + d)), over_heads(mask[d]), ALU.add))
                            link(dve.tensor_reduce(mx[:, d, g, :], heads(am), X, ALU.max))
                        tt(mx[:, :, g, :], mx[:, :, g, :], m0[:, :, g, :], ALU.max).then_inc(t_dve, 1)
                    elif kind == "decay":
                        for d in range(2):
                            ins = tt(heads(em[:, d, :]), over_heads(mask[1 - d]), heads(bank(T + d)), ALU.subtract)
                            if g == 0:
                                last = (P - 1) * (1 - d)
                                ins = tt(ws[:, d, :], ig[:, d, g, :], heads(bank(T + d))[:, :, last], ALU.subtract)
                        ins.then_inc(t_half, 1)
                        dve.wait_ge(t_act, l * NT + (n + 1))
                        dve.sem_inc(t_dve, 1)
                    elif kind == "turn":
                        dve.tensor_copy(qTa, bank(T)).then_inc(t_dve, 1)
                    elif kind == "scores":
                        for d in range(2):
                            ins = tt(em[:, d, :], em[:, d, :], bank(T), ALU.mult)
                        ins.then_inc(t_dve, 1)
                    elif kind == "read_f":
                        den = psum[:, T + 1, 0:8].rearrange("p (d h) -> p d h", d=2)
                        if g == 0:
                            link(dve.tensor_copy(dn, den))
                        else:
                            q_n = psum[:, T + 1, 8:16].rearrange("p (d h) -> p d h", d=2)
                            link(tt(dn, q_n, wi[:, :, g, :], ALU.mult))
                            link(tt(dn, den, dn, ALU.add))
                        link(ts(rr, dn, -1.0, None, ALU.mult))
                        link(tt(dn, dn, rr, ALU.max))
                        link(tt(dn, dn, ex[:, :, g, :], ALU.max))
                        link(dve.reciprocal(rr, dn))
                        if g == 1:
                            link(tt(wi[:, :, g, :], wi[:, :, g, :], rr, ALU.mult))
                        tt(heads(hs), heads(bank(T)), over_cols(rr[:, 0, :]), ALU.mult).then_inc(t_dve, 1)
                    elif kind in ("read_b", "inter_b"):
                        terms = [(T, rr[:, 1, :])] + [(T + 1, wi[:, 0, 1, :])] * g if kind == "read_b" else [(T, wi[:, 1, 1, :])]
                        for j, (b, s) in enumerate(terms):
                            link(tt(heads(am), heads(bank(b)), over_cols(s), ALU.mult))
                            ins = tt(hs, hs, am, ALU.add)
                            if j < len(terms) - 1:
                                link(ins)
                        ins.then_inc(t_dve, 1)
                    elif kind == "gate":
                        dve.wait_ge(t_act, l * NT + (n + 1))
                        link(ts(am, am, 1.0, None, ALU.add))
                        link(dve.reciprocal(am, am))
                        tt(ch[:, g, AO, :], am, hs, ALU.mult).then_inc(t_dve, 1)
                    elif kind == "na_turn":
                        dve.tensor_copy(na_kT, bank(T + 1)).then_inc(t_dve, 1)
                    elif kind == "na_cache":
                        dve.tensor_copy(na_cT, bank(T)).then_inc(t_dve, 1)
                    elif kind == "na_scores":
                        s = [heads(na_s[:, 0, :]), heads(na_s[:, 1, :])]
                        if g == 0:
                            link(dve.tensor_reduce(n_mx, heads(bank(T)), X, ALU.max))
                            tt(s[0], heads(bank(T)), over_cols(n_mx), ALU.subtract).then_inc(t_half, 1)
                        else:
                            dve.tensor_reduce(n_mb, heads(bank(T + 1)), X, ALU.max)
                            link(tt(s[0], heads(bank(T)), heads(rpb[:, i, :]), ALU.add))
                            link(dve.tensor_reduce(n_mx, s[0], X, ALU.max))
                            link(tt(n_mx, n_mx, n_mb, ALU.max))
                            tt(s[0], s[0], over_cols(n_mx), ALU.subtract)
                            tt(s[1], heads(bank(T + 1)), over_cols(n_mx), ALU.subtract).then_inc(t_half, 1)
                        dve.wait_ge(t_act, l * NT + (n + 1))
                        link(dve.tensor_reduce(n_sum[:, 0, :], s[0], X, ALU.add))
                        if g == 1:
                            link(dve.tensor_reduce(n_sum[:, 1, :], s[1], X, ALU.add))
                            link(tt(n_sum[:, 0, :], n_sum[:, 0, :], n_sum[:, 1, :], ALU.add))
                        dve.reciprocal(n_sum[:, 0, :], n_sum[:, 0, :]).then_inc(t_dve, 1)
                    elif kind == "na_probs":
                        dve.tensor_copy(na_pT[:, 0, :], bank(T)).then_inc(t_dve, 1)
                    elif kind == "na_out":
                        o = ch[:, g, BQ, :].rearrange("p (j a n) -> p j a n", j=4, a=2)[:, :, i, :]
                        tt(o, psum[:, T, 0:4 * NAD].rearrange("p (j n) -> p j n", j=4), over_cols(n_sum[:, 0, :], NAD), ALU.mult)\
                            .then_inc(t_dve, 1)
                    else:
                        dve.sem_inc(t_dve, 1)

                def sigmoid(m):
                    dve.wait_ge(sig_exp, l * 12 + (m + 1))
                    link(ts(sig, sig, 1.0, None, ALU.add))
                    dve.reciprocal(ch[:, m % 2, GATE_BUF[m // 2], :], sig).then_inc(sig_done, 1)

                for q in range(QUARTERS):
                    in_order(h_round, t_round, q)
                    c, g = q // 4, (q // 2) % 2
                    if q % 2:
                        if g:
                            dve.wait_ge(slot_used, used(l, N_MOD + c))
                        else:
                            dve.wait_ge(proj_filled, l * N_IN + (c + 1))
                            dve.wait_ge(bias_loaded[c % RING], l * (N_IN // RING * 16) + (c // RING + 1) * 16)
                        tt(ch[:, g, c if c < 12 else GATE_BUF[c - 12], :], bank(PJ + g), bias_ring[:, c % RING, :], ALU.add)\
                            .then_inc(proj_read, 1)
                        if c >= 12 and (c, g) != (12, 0):
                            sigmoid((c - 12) * 2 + g - 1)
                sigmoid(11)
                for b in range(3):
                    for g in range(G):
                        for hf in range(2):
                            n = 2 * g + hf
                            if n == 3:
                                dve.wait_ge(slot_used, used(l, N_MOD + N_IN + b))
                            else:
                                dve.wait_ge(br_filled, l * 9 + (3 * b + n + 1))
                            gate = ch[:, g, GATE_BUF[2 * b + hf], :]
                            yh = y[:, g, hf * W:(hf + 1) * W]
                            if b == 0:
                                tt(yh, bank(n), gate, ALU.mult).then_inc(br_added, 1)
                            else:
                                dve.wait_ge(br_added, l * 12 + (4 * b + n))
                                link(tt(lnt[:, 0, 0:W], bank(n), gate, ALU.mult))
                                tt(yh, yh, lnt[:, 0, 0:W], ALU.add).then_inc(br_added, 1)

                def finish(sub):
                    for hf in range(2):
                        for g in range(G):
                            n = 4 * sub + 2 * hf + g
                            dve.wait_ge(grep_ready, l * 8 + (n + 1))
                            if sub == 0:
                                if g:
                                    dve.wait_ge(slot_used, used(l, N_MOD + N_IN + N_BR + hf))
                                else:
                                    dve.wait_ge(out_filled, l * 2 + (hf + 1))
                                src = bank(2 * hf + g)
                            else:
                                src = y_moe[:, g, hf * W:(hf + 1) * W]
                            xh = x[:, g, hf * W:(hf + 1) * W]
                            dve.wait_ge(out_added, l * 8 + (n + 1))
                            link(tt(lnt[:, 0, 0:W], src, grep, ALU.mult))
                            stt(out=xh, in0=xh, scalar=ALPHA, in1=lnt[:, 0, 0:W], op0=ALU.mult, op1=ALU.add).then_inc(out_added, 1)
                    dve.wait_ge(out_added, l * 8 + (4 * sub + 5))
                    dve.wait_ge(ln_loaded, l * 32 + (16 * sub + 16))
                    for g in range(G):
                        for hf in range(2):
                            link(dve.bn_stats(bn6[:, hf, :], x[:, g, hf * W:(hf + 1) * W]), dve_tick)
                        link(dve.bn_aggr(bn2, bn6.rearrange("p a b -> p (a b)")))
                        ts(rstd, bn2[:, 1:2], LN_EPS, None, ALU.add).then_inc(ln_var, 1)
                        dve.wait_ge(ln_rstd, l * 4 + (2 * sub + g + 1))
                        link(ts(x[:, g, :], x[:, g, :], bn2[:, 0:1], rstd, ALU.subtract, ALU.mult))
                        link(tt(x[:, g, :], x[:, g, :], lnb[:, 0, :], ALU.mult))
                        ins = tt(x[:, g, :], x[:, g, :], lnb[:, 1, :], ALU.add)
                        if g:
                            ins.then_inc(x_ready, 1)
                        else:
                            link(ins)

                finish(0)
                modulate(1)
                dve.wait_ge(rt_filled, l + 1)
                link(dve.tensor_copy(lg.rearrange("p g n -> p (g n)"), psum[:, T, 0:40]))

                def first_max(sel, val, mx_):
                    link(dve.tensor_reduce(mx_, val, X, ALU.max))
                    link(tt(sel, val, mx_.unsqueeze(2).to_broadcast([P, G, 4]), ALU.is_equal))
                    link(dve.tensor_copy(r_pre, sel[:, :, 0]))
                    for j in range(1, 4):
                        link(dve.tensor_copy(r_w, sel[:, :, j]))
                        link(tt(sel[:, :, j], sel[:, :, j], r_pre, ALU.is_gt))
                        link(tt(r_pre, r_pre, r_w, ALU.max))

                first_max(r_sel, lg[:, :, 0:4], r_mx)
                tt(r_d, lg[:, :, 0:4], r_mx.unsqueeze(2).to_broadcast([P, G, 4]), ALU.subtract).then_inc(rt_half, 1)
                link(tt(r_x, lg[:, :, 4:20].rearrange("p g (a b) -> p g a b", a=4), r_sel.unsqueeze(3).to_broadcast([P, G, 4, 4]), ALU.mult))
                link(tt(r_le, r_x[:, :, 0, :], r_x[:, :, 1, :], ALU.add))
                link(tt(r_le, r_le, r_x[:, :, 2, :], ALU.add))
                link(tt(r_le, r_le, r_x[:, :, 3, :], ALU.add))
                first_max(r_o1, r_le, r_m1)
                link(stt(out=r_le, in0=r_o1, scalar=NEG, in1=r_le, op0=ALU.mult, op1=ALU.add))
                first_max(r_o2, r_le, r_m2)
                tt(r_e, r_m2, r_m1, ALU.subtract).then_inc(rt_half, 1)
                dve.wait_ge(rt_exp, l * 2 + 1)
                link(dve.tensor_reduce(r_p, r_d, X, ALU.add))
                link(dve.reciprocal(r_p, r_p))
                dve.wait_ge(rt_exp, l * 2 + 2)
                link(ts(r_w, r_e, 1.0, None, ALU.add))
                link(dve.reciprocal(r_w, r_w))
                link(tt(r_w, r_w, r_p, ALU.mult))
                link(tt(r_e, r_e, r_w, ALU.mult))
                link(tt(r_o1, r_o1, r_w.unsqueeze(2).to_broadcast([P, G, 4]), ALU.mult))
                link(tt(r_o2, r_o2, r_e.unsqueeze(2).to_broadcast([P, G, 4]), ALU.mult))
                link(tt(r_in, r_o1, r_o2, ALU.add))
                for g in range(G):
                    link(tt(gw[:, g, :].rearrange("p (a b) -> p a b", a=4), r_sel[:, g, :].unsqueeze(2).to_broadcast([P, 4, 4]),
                            r_in[:, g, :].unsqueeze(1).to_broadcast([P, 4, 4]), ALU.mult))
                link(dve.memset(y_moe, 0.0))
                dve.sem_inc(gate_ready, 1)
                dve.sem_inc(ldata_free, 1)
                with dve.Fori(0, NE) as e:
                    i = l * NE + e
                    mlink = Chain(dve, moe_chain, 6, i)
                    for g in range(G):
                        dve.wait_ge(up_exp, i * 2 + (g + 1))
                        den = den_e[:, g, :]
                        mlink(ts(den, den, 1.0, None, ALU.add))
                        mlink(dve.reciprocal(den, den))
                        mlink(tt(den, den, bank(2 * g), ALU.mult))
                        dve.wait_ge(hid_turned, i * 2 + (g + 1))
                        tt(hid[:, g, :], den, bank(2 * g + 1), ALU.mult).then_inc(hid_ready, 1)
                    for g in range(G):
                        for hf in range(2):
                            n = 2 * g + hf
                            if n == 3:
                                dve.wait_ge(slot_used, l * SLOTS + e * 3 + (RING + FIRST_EXPERT_SLOT + 3))
                            else:
                                dve.wait_ge(down_filled, i * 3 + (n + 5))
                            yh = y_moe[:, g, hf * W:(hf + 1) * W]
                            stt(out=yh, in0=bank(6 + hf), scalar=gw[:, g, bass.ds(e, 1)], in1=yh, op0=ALU.mult, op1=ALU.add)\
                                .then_inc(down_added, 1)
                    mlink.close()
                dve.wait_ge(down_added, l * (4 * NE) + (4 * NE + 2))
                finish(1)
                dve.wait_ge(x_ready, l * 2 + 3)
                link.close()

        @block.gpsimd
        def _(pool):
            tt = pool.tensor_tensor
            pool.wait_ge(start_loaded, 48)
            with pool.Fori(0, DEPTH) as l:
                link = Chain(pool, pool_chain, 64, l)
                pool.wait_ge(ldata_loaded, l * 32 + 32)

                def h_round(n):
                    kind, g, i = H_ROUNDS[n]
                    pool.wait_ge(h_pe, l * NH + (n + 1))
                    if kind == "prep":
                        pool.wait_ge(h_sigmoid, l * G + (g + 1))
                        s, t = decay, k_dec
                        link(tt(t, s, lb[:, :, :], ALU.mult))
                        link(tt(s, s, t, ALU.subtract))
                        link(tt(s, s, lb[:, :, :], ALU.add), pool_tick)
                        pool.tensor_scalar(ch[:, g, CF_F:CF_B + 1, :], s, -1.0, 1.0, ALU.mult, ALU.add)
                        link(pool.tensor_scalar(t, s, TINY, None, ALU.max), pool_tick)
                        pool.tensor_copy(s, t).then_inc(h_forget, 1)
                        pool.wait_ge(h_act, l * NH + (n + 1))
                        pool.sem_inc(h_pool, 1)
                    elif kind == "turn":
                        pool.wait_ge(h_act, l * NH + (n + 1))
                        tt(k_dec[:, 0, :], k_T[:, 0, :], k_T[:, 1, :], ALU.add).then_inc(h_pool, 1)
                    elif kind == "level":
                        pool.wait_ge(h_act, l * NH + (n + 1))
                        if i < NL:
                            tt(k_dec, k_T, decay, ALU.mult).then_inc(h_pool, 1)
                        elif g == 0:
                            tt(k_dec, ch[:, 0, CF_F:CF_B + 1, :], decay, ALU.mult).then_inc(h_pool, 1)
                        else:
                            pool.sem_inc(h_pool, 1)
                    else:
                        pool.sem_inc(h_pool, 1)

                def diagonal(v, g):
                    for d in range(2):
                        ins = tt(heads(dg[:, d, :]), over_heads(ident), over_cols(v[:, d, g, :]), ALU.mult)
                    return ins

                def t_round(n):
                    kind, g, i = T_ROUNDS[n]
                    pool.wait_ge(t_pe, l * NT + (n + 1))
                    nxt = T_ROUNDS[n + 1] if n + 1 < NT else None
                    if nxt and nxt[0] == "max":
                        pool.wait_ge(t_dve, l * NT + (n + 1))
                        diagonal(ig, nxt[1]).then_inc(t_pool, 1)
                    elif kind == "max":
                        pool.wait_ge(t_dve, l * NT + (n + 1))
                        tt(mt[:, :, g, :], bc[:, :, g, :], mx[:, :, g, :], ALU.add)
                        tt(wi[:, :, g, :], m0[:, :, g, :], mx[:, :, g, :], ALU.subtract)
                        diagonal(mx, g).then_inc(t_pool, 1)
                    elif kind == "decay" and g == 1:
                        pool.wait_ge(proj_read, proj(l, AK, 1))
                        halves_ = lambda v: v.rearrange("p (h a b n) -> p h a b n", h=4, a=2, b=2)
                        sin = c_("sin").rearrange("p (a b n) -> p a b n", a=2, b=2)
                        for c in (AQ, AK):
                            v = ch[:, 1, c, :]
                            tt(heads(am), heads(v), over_heads(c_("cos")), ALU.mult)
                            for b in range(2):
                                ins = tt(halves_(hs)[:, :, :, b, :], halves_(v)[:, :, :, 1 - b, :],
                                         sin[:, :, b, :].unsqueeze(1).to_broadcast([P, 4, 2, 32]), ALU.mult)
                            link(ins)
                            ins = tt(v, am, hs, ALU.add)
                            if c == AQ:
                                link(ins)
                        ins.then_inc(t_pool, 1)
                    elif kind == "read_b" and g == 0:
                        pool.sem_inc(pool_tick, 1)
                        link(pool.tensor_scalar(ws, ws, QSCALE, None, ALU.mult))
                        for d in range(2):
                            ins = tt(heads(dg[:, d, :]), heads(ch[:, 0, AK, :]), over_cols(ws[:, d, :]), ALU.mult)
                        ins.then_inc(t_pool, 1)
                    else:
                        pool.sem_inc(t_pool, 1)

                for q in range(QUARTERS):
                    in_order(h_round, t_round, q)
                link.close()


def constants():
    i = np.arange(P)
    c = np.zeros((P, N_CONST), np.float32)

    def put(name, v):
        a, n = CONST[name]
        c[:, a:a + n] = np.asarray(v, np.float32).reshape(P, n)

    row, col = i[:, None], i[None, :]
    put("ident", row == col)
    put("ones", np.ones((P, P)))
    put("tri_f", row <= col)
    put("tri_b", row >= col)
    put("rest_f", row > col)
    put("rest_b", row < col)
    put("below", np.where(col <= row, 0.0, NEG))
    put("above", np.where(col >= row, 0.0, NEG))
    lv = np.zeros((2, P, NL, P), np.float32)
    masks = np.zeros((P, 2, NL, P), np.uint8)
    for n, h in enumerate(LEVELS):
        mid = col // (2 * h) * (2 * h) + h
        right = col >= mid
        lv[0, :, n] = np.where(right, (row >= mid) & (row <= col), (row > col) & (row < mid))
        lv[1, :, n] = np.where(right, (row >= mid) & (row < col), (row >= col) & (row < mid))
        same = row // (2 * h) == col // (2 * h)
        masks[:, 0, n] = same & (row < mid) & (col >= mid)
        masks[:, 1, n] = same & (row >= mid) & (col < mid)
    put("level_mask", masks.reshape(P, -1).view(np.float32))
    put("level_f", lv[0])
    put("level_b", lv[1])
    quarter = DK // 4
    inv = (np.float32(10000.0) ** (-np.arange(0, DK // 2, 2, dtype=np.float32) / np.float32(DK // 2))).astype(np.float32)
    cos, sin = np.zeros((P, 2, 2, quarter), np.float32), np.zeros((P, 2, 2, quarter), np.float32)
    for a, pos in enumerate((i // GRID_W, i % GRID_W)):
        ang = pos.astype(np.float32)[:, None] * inv[None, :]
        cos[:, a, 0] = cos[:, a, 1] = np.cos(ang)
        sin[:, a, 0], sin[:, a, 1] = -np.sin(ang), np.sin(ang)
    put("cos", cos)
    put("sin", sin)
    return c


def bias_index():
    t = np.arange(P)
    r, c = t // GRID_W, t % GRID_W
    start = np.clip(c - 8, 0, GRID_W - 16)
    inside = (c[None, :] >= start[:, None]) & (c[None, :] < start[:, None] + 16)
    dr = r[None, :] - r[:, None] + 7
    dc = np.clip(c[None, :] - c[:, None] + 15, 0, 30)
    return np.where(inside, dr * 31 + dc, -1)


def kernel(**inputs):
    import concourse.bacc as bacc
    from concourse.bass_utils import run_bass_kernel_spmd

    v = {k: np.asarray(a) for k, a in inputs.items()}

    def tiles(w, k):
        return w.reshape(k, P, -1).transpose(1, 0, 2).reshape(P, -1)

    def rep(a):
        return np.broadcast_to(a.reshape(1, -1), (P, a.size))

    stream = np.zeros((DEPTH, SLOTS, P, SLOT), np.float32)
    b_in = np.zeros((DEPTH, N_IN, P, W), np.float32)
    ldata = np.zeros((DEPTH, P, N_LDATA), np.float32)
    ln = np.zeros((DEPTH, 2, P, 2, D), np.float32)
    where = bias_index()
    for l in range(DEPTH):
        for c in range(N_MOD):
            stream[l, c] = tiles(v["w_mod"][l][:, c * W:(c + 1) * W], KT)
        for c in range(N_IN):
            cols = slice(CHUNK_COL[c], CHUNK_COL[c] + W)
            stream[l, N_MOD + c] = tiles(v["w_in"][l][:, cols], KT)
            b_in[l, c] = rep(v["b_in"][l, cols])
        for b in range(N_BR):
            stream[l, N_MOD + N_IN + b] = tiles(v["w_branch"][l, b], BT)
        for b in range(N_OUT):
            stream[l, N_MOD + N_IN + N_BR + b] = tiles(v["w_out"][l][:, b * W:(b + 1) * W], KT)
        for e in range(NE):
            stream[l, FIRST_EXPERT_SLOT + 3 * e] = tiles(v["w_e1"][l, e], KT)
            stream[l, FIRST_EXPERT_SLOT + 3 * e + 1] = tiles(v["w_e3"][l, e], KT)
            stream[l, FIRST_EXPERT_SLOT + 3 * e + 2] = tiles(v["w_e2"][l, e], BT)

        def put(name, a):
            at, n = LDATA[name]
            ldata[l, :a.shape[0], at:at + n] = a.reshape(a.shape[0], n)

        put("C0", v["state_mlstm_C"][0, l].transpose(2, 0, 1, 3))
        put("S0", v["state_hgrn"][0, l].transpose(2, 0, 1, 3))
        bias = v["na_rpb"][l].reshape(NAH, -1)[:, np.maximum(where, 0)]
        bias = np.where(where[None] >= 0, bias, np.float32(NEG))
        put("rpb", bias.reshape(4, 2, P, P).transpose(2, 1, 0, 3))
        put("ck", v["cache_na_k"][0, l].transpose(1, 0, 2))
        put("cv", v["cache_na_v"][0, l].transpose(1, 0, 2))
        gates = slice(GATES_COL, GATES_COL + 16)
        put("w_gates", tiles(v["w_in"][l][:, gates], KT))
        put("w_route", tiles(np.concatenate([v["w_rg"][l], v["w_re"][l]], 1), KT))
        put("b_gates", rep(v["b_in"][l, gates]))
        put("fbias", rep(v["mlstm_fbias"][l]))
        put("n0", v["state_mlstm_n"][0, l].transpose(2, 0, 1))
        m0 = np.zeros((P, 2, G, 4), np.float32)
        m0[:, :, 1, :] = v["state_mlstm_m"][0, l][None]
        put("m0", m0)
        bm = v["b_mod"][l].reshape(6, 2, 4, P)
        put("b_mod", np.concatenate([bm[s].reshape(8, P) for s in (0, 1, 3, 4)]).T)
        rows = np.zeros((8, W), np.float32)
        for s, vec in enumerate((2, 5)):
            for hf in range(2):
                rows[4 * s + 2 * hf:4 * s + 2 * hf + 2] = bm[vec, hf].reshape(1, W)
        put("b_rows", rows)
        past = np.zeros((P, DEPTH), np.float32)
        past[:, 1:l + 1] = 1.0
        put("past", past)
        for s in range(2):
            ln[l, s, :, 0] = v["ln_g"][l, s]
            ln[l, s, :, 1] = v["ln_b"][l, s]
    const = constants()
    arrays = {
        "const": const,
        "x": np.stack([v["x_prompt"][0], v["x_sample"][0]], 1),
        "c_cols": np.stack([v["c_ctx"].reshape(KT, P), v["c"][0].reshape(KT, P)], 2).transpose(1, 0, 2),
        "stream": stream.reshape(DEPTH * SLOTS, P, SLOT),
        "b_in": b_in.reshape(DEPTH * N_IN, P, W),
        "ldata": ldata,
        "ln": ln.reshape(DEPTH * 2, P, 2, D),
        "lb_logits": np.broadcast_to(v["hgrn_lb_logits"][None], (P, 2, DEPTH, W)),
    }
    arrays = {f"in_{k}": np.ascontiguousarray(a) for k, a in arrays.items()}
    outs = {"y": (G, P, D), "na_k": (DEPTH, NAH, P, NAD), "na_v": (DEPTH, NAH, P, NAD), "C": (DEPTH, 2, HEADS, DK, DK),
            "n": (DEPTH, 1, 2 * HEADS * DK), "m": (DEPTH, 2, HEADS), "hgrn": (DEPTH, 2, HEADS, DK, DK)}
    nc = bacc.Bacc("TRN2", target_bir_lowering=False, num_devices=1)
    dram = {k[3:]: nc.dram_tensor(k, a.shape, mybir.dt.from_np(a.dtype), kind="ExternalInput").ap() for k, a in arrays.items()}
    out = {k: nc.dram_tensor(f"out_{k}", s, F32, kind="ExternalOutput").ap() for k, s in outs.items()}
    build(nc, dram, out)
    r = run_bass_kernel_spmd(nc, [arrays], core_ids=[0]).results[0]
    r = {k: r[f"out_{k}"] for k in outs}
    return (r["y"][0][None], r["y"][1][None], r["na_k"][None], r["na_v"][None], r["C"][None],
            r["n"].reshape(1, DEPTH, 2, HEADS, DK), r["m"][None], r["hgrn"][None])
```

```python
from contextlib import ExitStack

import numpy as np

import concourse.bass as bass
from concourse import mybir

F32 = mybir.dt.float32
U8 = mybir.dt.uint8
I32 = mybir.dt.int32
ALU = mybir.AluOpType
ACT = mybir.ActivationFunctionType
X = mybir.AxisListType.X

P = 128
D = 1024
DEPTH = 2
G = 2
KT = D // P
W = 512
HEADS = 4
DK = 128
NAH, NAD = 8, 64
BT = W // P
NE = 16
FE = 512
GRID_W = 64
NEG = -1.0e30
TINY = 1.0e-19
LN_EPS, RMS_EPS = 1e-5, 1e-6
ALPHA = (2 * DEPTH) ** 0.25
QSCALE = DK ** -0.5
NSCALE = NAD ** -0.5

RING = 3
SLOT = KT * W
N_MOD, N_IN, N_BR, N_OUT = 12, 18, 3, 2
FIRST_EXPERT_SLOT = N_MOD + N_IN + N_BR + N_OUT + 1
SLOTS = FIRST_EXPERT_SLOT + 3 * NE
CAP = P // 2
PASSES = G * P // CAP
STEPS = PASSES * NE
USES = SLOTS + (PASSES - 1) * 3 * NE
assert FIRST_EXPERT_SLOT % RING == 0 and SLOTS % RING == 0 and N_MOD % RING == 0

CF_F, CF_B, CQ, CI, AQ, AK, AV, AO, BQ, BK, BV, CG = range(12)
CHUNK_COL = [3600, 4112, 4624, 5136, 0, 512, 1024, 1536, 2064, 2576, 3088, 5648] + [6160 + W * j for j in range(6)]
GATES_COL = 2048
GATE_BUF = [CF_F, CF_B, CQ, CI, AQ, AK]
LEVELS = [64, 32, 16, 8, 4, 2, 1]
NL = len(LEVELS)

MOD_COLS = {0: 0, 1: 4, 2: 8, 3: 12, 6: 16, 7: 20, 8: 24, 9: 28}
MOD_ROWS = {4: 0, 5: 1, 10: 2, 11: 3}
SHIFT, SCALE = (0, 16), (8, 24)



def fields(sizes):
    at, out = 0, {}
    for name, n in sizes:
        out[name] = (at, n)
        at += n
    return out, at


CONST, N_CONST = fields([("ident", P), ("ones", P), ("tri_f", P), ("tri_b", P), ("rest_f", P), ("rest_b", P),
                         ("below", P), ("above", P), ("level_f", NL * P), ("level_b", NL * P),
                         ("cos", P), ("sin", P), ("iota", CAP),
                         ("level_mask", 2 * NL * P // 4)])
LDATA, N_LDATA = fields([("C0", 2 * W), ("S0", 2 * W), ("rpb", 2 * W), ("ck", W), ("cv", W), ("w_gates", KT * 16),
                         ("w_route", KT * 20), ("b_gates", 16), ("fbias", 8), ("n0", 8), ("m0", 16), ("b_mod", 32),
                         ("b_rows", W), ("past", DEPTH)])

H_ROUNDS = []
for _g in range(G):
    H_ROUNDS += [("prep", _g, 0), ("turn", _g, 0)] + [("level", _g, i) for i in range(NL + 1)] + [("out", _g, 0)]
H_ROUNDS += [("gate", 0, 0), ("gate", 1, 0)]
T_ROUNDS = [("forget", 0, 0), ("cumsum", 0, 0)]
for _g in range(G):
    T_ROUNDS += [("max", _g, 0), ("decay", _g, 0), ("turn", _g, 0), ("scores", _g, 0), ("read_f", _g, 0), ("read_b", _g, 0)]
    T_ROUNDS += [("state", 0, 0), ("norm_state", 0, 0)] if _g == 0 else [("inter_b", 1, 0)]
    T_ROUNDS += [("gate", _g, 0)]
for _g in range(G):
    T_ROUNDS += [("na_turn", _g, 0)] + [("na_cache", _g, 0)] * (_g == 1)
    for _p in range(2):
        T_ROUNDS += [("na_scores", _g, _p), ("na_probs", _g, _p), ("na_out", _g, _p)]
NH, NT = len(H_ROUNDS), len(T_ROUNDS)
QUARTERS = 4 * N_IN


def ready_quarter(chunk, g):
    return 4 * chunk + 2 * g + 2


def plan(rounds, first, needs):
    at, q = [], first
    for r in rounds:
        q = max([q] + [ready_quarter(c, g) for c, g in needs(r)])
        at.append(q)
        q += 1
    return at


def h_needs(r):
    kind, g, _ = r
    return {"prep": [(CQ, g)], "out": [(CI, g)], "gate": [(CG, g)]}.get(kind, [])


def t_needs(r):
    kind, g, _ = r
    return {"turn": [(AK, g)], "read_f": [(AV, g)], "gate": [(AO, g)], "na_turn": [(BK, g)], "na_out": [(BV, g)]}.get(kind, [])


H_AT = plan(H_ROUNDS, 0, h_needs)
T_AT = plan(T_ROUNDS, 12, t_needs)
assert max(H_AT + T_AT) < QUARTERS
assert all(ready_quarter(12 + j, 0) - 1 > (H_AT[-3] if j < 4 else T_AT[T_ROUNDS.index(("gate", 1, 0))]) for j in range(6))



def build(nc, dram, out):
    ctx = ExitStack()
    with ctx:
        def sb(name, shape, dt=F32):
            return ctx.enter_context(nc.sbuf_tensor(name, shape, dt))

        def sem(name):
            return ctx.enter_context(nc.semaphore(name))

        ring = sb("ring", [P, RING, SLOT])
        bias_ring = sb("bias_ring", [P, RING, W])
        fullest = sb("fullest", [P, 1], I32)
        const = sb("const", [P, N_CONST])
        ldata = sb("ldata", [P, N_LDATA])
        x = sb("x", [P, G, D])
        hT = sb("hT", [P, KT, G * P])
        ch = sb("ch", [P, G, 12, W])
        lb = sb("lb", [P, 2, W])
        scT = sb("scT", [P, KT, G])
        scZ = sb("scZ", [P, KT, 4, 8])
        mod = sb("mod", [P, 32, G])
        grow = sb("grow", [8, W])
        hbuf = sb("hbuf", [P, 13 * W])
        o_norm = sb("o_norm", [P, G, W])
        tbuf = sb("tbuf", [P, 8 * W])
        sm = sb("sm", [P, 640])

        log_f = hbuf[:, 0:2 * W].rearrange("p (d n) -> p d n", d=2)
        k_T = hbuf[:, 2 * W:4 * W].rearrange("p (d n) -> p d n", d=2)
        decay = hbuf[:, 4 * W:6 * W].rearrange("p (d n) -> p d n", d=2)
        q_dec = hbuf[:, 6 * W:8 * W].rearrange("p (d n) -> p d n", d=2)
        k_dec = hbuf[:, 8 * W:10 * W].rearrange("p (d n) -> p d n", d=2)
        q_T = hbuf[:, 10 * W:11 * W]
        att = hbuf[:, 11 * W:12 * W]
        o_sb = hbuf[:, 12 * W:13 * W]
        hsig = hbuf[:, 4 * W:7 * W]
        y = hbuf[:, 0:4 * W].rearrange("p (g n) -> p g n", g=G)
        lnb = hbuf[:, 4 * W:8 * W].rearrange("p (a n) -> p a n", a=2)
        grep = hbuf[:, 8 * W:9 * W]
        lnt = hbuf[:, 9 * W:13 * W].rearrange("p (g n) -> p g n", g=G)
        brT = tbuf[:, 0:4 * W].rearrange("p (b k t) -> p b k t", b=2, k=BT)

        em = tbuf[:, 0:2 * W].rearrange("p (d n) -> p d n", d=2)
        dg = tbuf[:, 2 * W:4 * W].rearrange("p (d n) -> p d n", d=2)
        am = tbuf[:, 4 * W:5 * W]
        qTa = tbuf[:, 5 * W:6 * W]
        kTa = tbuf[:, 6 * W:7 * W]
        hs = tbuf[:, 7 * W:8 * W]
        na_s, na_pT, na_cT, na_qT, na_kT = em, dg, am, qTa, kTa
        chf = ch[:, :, :, :].rearrange("p g c n -> p (g c n)")
        y_moe = chf[:, 0:4 * W].rearrange("p (g n) -> p g n", g=G)
        h2tok = chf[:, 4 * W:8 * W].rearrange("p (g n) -> p g n", g=G)
        lb_e = chf[:, 10 * W:14 * W].rearrange("p (d j n) -> p d j n", d=2, j=DEPTH)
        lb_m = chf[:, 14 * W:16 * W].rearrange("p (d n) -> p d n", d=2)

        xs = tbuf[:, 0:W]
        xgT = tbuf[:, W:2 * W].rearrange("p (k s) -> p k s", k=KT)
        esig = tbuf[:, 2 * W:2 * W + FE // 2]
        ehid = tbuf[:, 2 * W + FE // 2:3 * W]
        ehidT = tbuf[:, 3 * W:3 * W + FE // 2]
        e_sel = tbuf[:, 3 * W + FE // 2:4 * W].rearrange("p (g n) -> p g n", g=G)
        e_out = tbuf[:, 4 * W:5 * W]
        e_selT = tbuf[:, 5 * W:5 * W + G * P].rearrange("p (g n) -> p g n", g=G)
        e_pick = tbuf[:, 5 * W + G * P:5 * W + G * P + G * CAP].rearrange("p (g n) -> p g n", g=G)
        rank = tbuf[:, 6 * W:6 * W + G * NE].rearrange("p (g n) -> p g n", g=G)
        sent = tbuf[:, 6 * W + 32:6 * W + 32 + G * NE].rearrange("p (g n) -> p g n", g=G)
        total = tbuf[:, 6 * W + 64:6 * W + 64 + NE]
        most = tbuf[:, 6 * W + 80:6 * W + 81]

        small_at = [0]

        def small(*shape):
            n = int(np.prod(shape))
            a = small_at[0]
            small_at[0] += n
            v = sm[:, a:a + n]
            if len(shape) == 2:
                v = v.rearrange("p (a b) -> p a b", a=shape[0])
            if len(shape) == 3:
                v = v.rearrange("p (a b c) -> p a b c", a=shape[0], b=shape[1])
            return v

        ig = small(2, G, 4)
        fz = small(2, G, 4)
        fn = small(2, G, 4)
        lf = small(2, G, 4)
        bc = small(2, G, 4)
        mx = small(2, G, 4)
        mt = small(2, G, 4)
        wi = small(2, G, 4)
        ex = small(2, G, 4)
        dn = small(2, 4)
        rr = small(2, 4)
        ws = small(2, 4)
        h4 = small(4)
        h4b = small(4)
        n_mx = small(4)
        n_mb = small(4)
        n_sum = small(2, 4)
        bn6 = small(2, 6)
        bn2 = small(2)
        rstd = small(1)
        lg = small(G, 20)
        r_d = small(G, 4)
        r_mx, r_p, r_m1, r_m2, r_e, r_w = (small(G) for _ in range(6))
        r_pre = small(G)
        r_sel, r_o1, r_o2, r_le, r_eq, r_in = (small(G, 4) for _ in range(6))
        r_x = small(G, 4, 4)
        gw = small(G, NE)
        psum = ctx.enter_context(nc.psum_tensor("psum", [P, 8, W], F32))
        PJ, EX, PP, T = 0, 2, 4, 6
        SPREAD = [(6, 7), (3, 2)]

        def bank(b, n=1):
            return psum[:, b, :] if n == 1 else psum[:, b:b + n, :]

        def heads(ap):
            return ap.rearrange("p (h n) -> p h n", h=HEADS)

        def over_heads(ap):
            return ap.unsqueeze(1).to_broadcast([P, HEADS, P])

        def over_cols(ap, n=P):
            return ap.unsqueeze(2).to_broadcast([P, 4, n])

        def c_(name):
            a, n = CONST[name]
            return const[:, a:a + n]

        def l_(name):
            a, n = LDATA[name]
            return ldata[:, a:a + n]

        ident, ones = c_("ident"), c_("ones")
        level_mask = c_("level_mask").bitcast(U8).rearrange("p (d i n) -> p d i n", d=2, i=NL)
        tri = [c_("tri_f"), c_("tri_b")]
        rest = [c_("rest_f"), c_("rest_b")]
        mask = [c_("below"), c_("above")]
        level = [c_("level_f").rearrange("p (i n) -> p i n", i=NL), c_("level_b").rearrange("p (i n) -> p i n", i=NL)]
        C0 = l_("C0").rearrange("p (d h n) -> p d h n", d=2, h=HEADS)
        S0 = l_("S0").rearrange("p (d h n) -> p d h n", d=2, h=HEADS)
        sig = l_("b_rows")
        rpb = l_("rpb").rearrange("p (a n) -> p a n", a=2)
        w_gates = l_("w_gates").rearrange("p (k n) -> p k n", k=KT)
        w_route = l_("w_route").rearrange("p (k n) -> p k n", k=KT)
        m0 = l_("m0").rearrange("p (d g h) -> p d g h", d=2, g=G)

        start_loaded = sem("start_loaded")
        ldata_loaded = sem("ldata_loaded")
        ldata_free = sem("ldata_free")
        slot_loaded = [sem(f"slot_loaded{i}") for i in range(RING)]
        bias_loaded = [sem(f"bias_loaded{i}") for i in range(RING)]
        slot_used = sem("slot_used")
        ln_loaded = sem("ln_loaded")
        silu_c = sem("silu_c")
        exp_c = sem("exp_c")
        lb_max = sem("lb_max")
        lb_exp = sem("lb_exp")
        mod_ready = sem("mod_ready")
        x_ready = sem("x_ready")
        xt_filled = sem("xt_filled")
        xt_read = sem("xt_read")
        proj_filled = sem("proj_filled")
        proj_read = sem("proj_read")
        sig_exp = sem("sig_exp")
        sig_done = sem("sig_done")
        h_pe, h_act, h_dve, h_pool = sem("h_pe"), sem("h_act"), sem("h_dve"), sem("h_pool")
        t_pe, t_act, t_dve, t_pool = sem("t_pe"), sem("t_act"), sem("t_dve"), sem("t_pool")
        h_scores = sem("h_scores")
        h_exp = sem("h_exp")
        h_sigmoid = sem("h_sigmoid")
        h_forget = sem("h_forget")
        h_square = sem("h_square")
        t_half = sem("t_half")
        t_back = sem("t_back")
        br_turned = sem("br_turned")
        br_ready = sem("br_ready")
        br_filled = sem("br_filled")
        br_added = sem("br_added")
        yt_filled = sem("yt_filled")
        yt_ready = sem("yt_ready")
        out_filled = sem("out_filled")
        out_added = sem("out_added")
        grep_filled = sem("grep_filled")
        grep_ready = sem("grep_ready")
        ln_var = sem("ln_var")
        ln_rstd = sem("ln_rstd")
        rt_filled = sem("rt_filled")
        rt_half = sem("rt_half")
        rt_exp = sem("rt_exp")
        h2_turned = sem("h2_turned")
        h2_ready = sem("h2_ready")
        sent_ready = sem("sent_ready")
        ranked = sem("ranked")
        fullest_ready = sem("fullest_ready")
        rank_moved = sem("rank_moved")
        pick_ready = sem("pick_ready")
        gathered = sem("gathered")
        xs_ready = sem("xs_ready")
        xg_turned = sem("xg_turned")
        xg_ready = sem("xg_ready")
        up_exp = sem("up_exp")
        hid_ready = sem("hid_ready")
        hid_turned = sem("hid_turned")
        hidT_ready = sem("hidT_ready")
        sel_ready = sem("sel_ready")
        sel_turned = sem("sel_turned")
        selT_ready = sem("selT_ready")
        eout_ready = sem("eout_ready")
        spread = sem("spread")
        spread_added = sem("spread_added")
        dve_chain, pool_chain, act_chain = sem("dve_chain"), sem("pool_chain"), sem("act_chain")
        moe_chain = sem("moe_chain")
        dve_tick, pool_tick, act_tick, pe_tick, sp_tick = (sem(f"{n}_tick") for n in ("dve", "pool", "act", "pe", "sp"))
        ticks = {nc.vector: dve_tick, nc.scalar: act_tick, nc.tensor: pe_tick, nc.sync: sp_tick}
        kv_stored = sem("kv_stored")
        state_stored = sem("state_stored")
        hgrn_stored = sem("hgrn_stored")
        y_stored = sem("y_stored")
        N_STATE = 4 * 16

        class Chain:

            def __init__(self, eng, s, per, index=0):
                self.eng, self.s, self.per, self.index, self.n = eng, s, per, index, 0

            def __call__(self, ins, alone=None):
                self.n += 1
                ins.then_inc(self.s, 1)
                self.eng.wait_ge(self.s, self.index * self.per + self.n)
                if alone is not None:
                    self.eng.sem_inc(alone, 1)

            def close(self):
                assert self.n <= self.per, (self.s, self.n)
                if self.n < self.per:
                    self.eng.sem_inc(self.s, self.per - self.n)

        def proj(l, c, g):
            return l * (2 * N_IN) + (2 * RING + 2 * c + g + 1)

        def used(l, i):
            return l * USES + (RING + i + 1)

        def used_e(l, p, e, j):
            return l * USES + p * (3 * NE) + e * 3 + (RING + FIRST_EXPERT_SLOT + j + 1)

        def arrived_e(l, p, e):
            return l * (USES // RING * 16) + p * (NE * 16) + e * 16 + (FIRST_EXPERT_SLOT // RING + 1) * 16

        def step(l, p, e):
            return l * STEPS + p * NE + (e + 1)

        def credit(eng, counts):
            for s, per in counts:
                eng.sem_inc(s, per)

        PE_STEP = ((gathered, 1), (xg_turned, 1), (sel_turned, 1), (hid_turned, 1), (spread, 4))
        ACT_STEP = ((xs_ready, 1), (up_exp, 1), (selT_ready, 1), (hidT_ready, 1), (eout_ready, 1))
        DVE_STEP = ((pick_ready, 1), (sel_ready, 1), (xg_ready, 1), (hid_ready, 1), (spread_added, 4), (moe_chain, 3))

        def skip(eng, l, p, counts):
            for s, per in counts:
                eng.wait_ge(s, (l * PASSES + p) * (NE * per) + per)
                eng.sem_inc(s, NE * per)

        def further_passes(eng, l, one_pass, otherwise):
            eng.wait_ge(fullest_ready, l + 1)
            eng.sem_inc(ticks[eng], 1)
            n = eng.value_load(fullest[0:1, 0:1], min_val=0, max_val=G * P)
            with eng.Fori(1, PASSES) as p:
                with eng.If(n > p * CAP):
                    one_pass(p)
                with eng.Else():
                    otherwise(p)

        def arrived(l, i):
            return l * (USES // RING * 16) + (i // RING + 1) * 16

        N_HALF = {"forget": 2, "decay": 1, "na_scores": 1}
        half_before = [sum(N_HALF.get(r[0], 0) for r in T_ROUNDS[:n]) for n in range(NT)]
        halves = sum(N_HALF.get(r[0], 0) for r in T_ROUNDS)

        def half(l, n, i=0):
            return l * halves + (half_before[n] + i + 1)

        def in_order(h_round, t_round, q):
            for n in range(NH):
                if H_AT[n] == q:
                    h_round(n)
            for n in range(NT):
                if T_AT[n] == q:
                    t_round(n)

        T_CHUNK = {(kind, g): c for g in range(G) for kind, c in (("turn", AK), ("read_f", AV), ("na_turn", BK), ("na_out", BV))}

        block = ctx.enter_context(nc.Block())

        @block.sync
        def _(sp):
            for dst, src in ((const[:, :], dram["const"]), (x[:, :, :], dram["x"]), (scT[:, :, :], dram["c_cols"])):
                sp.dma_start(dst, src).then_inc(start_loaded, 16)

            def load(l, i, j):
                sp.wait_ge(slot_used, l * USES + (i + 1))
                sp.dma_start(ring[:, j, :], dram["stream"][l * SLOTS + i]).then_inc(slot_loaded[j], 16)

            with sp.Fori(0, DEPTH) as l:
                sp.wait_ge(ldata_free, l + 1)
                sp.dma_start(lb_e, dram["lb_logits"]).then_inc(ldata_loaded, 16)
                sp.dma_start(ldata[:, :], dram["ldata"][l]).then_inc(ldata_loaded, 16)
                for i in range(N_MOD):
                    load(l, i, i % RING)
                for c in range(N_IN):
                    load(l, N_MOD + c, c % RING)
                    sp.wait_ge(proj_read, l * (2 * N_IN) + (2 * c + 2))
                    sp.dma_start(bias_ring[:, c % RING, :], dram["b_in"][l * N_IN + c]).then_inc(bias_loaded[c % RING], 16)
                for i in range(N_MOD + N_IN, FIRST_EXPERT_SLOT):
                    load(l, i, i % RING)
                    if i == N_MOD + N_IN:
                        sp.wait_ge(h_dve, l * NH + NH)
                        sp.wait_ge(h_act, l * NH + NH)
                        sp.wait_ge(h_pool, l * NH + NH)
                        sp.wait_ge(state_stored, l * N_STATE + N_STATE)
                        sp.dma_start(lnb, dram["ln"][l * 2]).then_inc(ln_loaded, 16)
                sp.wait_ge(x_ready, l * 2 + 2)
                sp.dma_start(lnb, dram["ln"][l * 2 + 1]).then_inc(ln_loaded, 16)

                def expert_pass(p):
                    with sp.Fori(0, NE) as e:
                        for j in range(3):
                            sp.wait_ge(slot_used, used_e(l, p, e, j - RING))
                            sp.dma_start(ring[:, j, :], dram["stream"][l * SLOTS + e * 3 + (FIRST_EXPERT_SLOT + j)])\
                              .then_inc(slot_loaded[j], 16)

                def no_pass(p):
                    for j in range(3):
                        sp.wait_ge(slot_loaded[j], arrived_e(l, p, -1))
                        sp.sem_inc(slot_loaded[j], 16 * NE)

                expert_pass(0)
                further_passes(sp, l, expert_pass, no_pass)
            sp.wait_ge(x_ready, 2 * DEPTH + 1)
            for g in range(G):
                sp.dma_start(out["y"][g], x[:, g, :]).then_inc(y_stored, 16)
            sp.wait_ge(y_stored, 16 * G)
            sp.wait_ge(kv_stored, 32 * DEPTH)
            sp.wait_ge(state_stored, N_STATE * DEPTH)
            sp.wait_ge(hgrn_stored, 16 * DEPTH)

        @block.tensor
        def _(pe):
            pe.sem_inc(slot_used, RING)
            credit(pe, PE_STEP)
            pe.wait_ge(start_loaded, 48)
            pe.wait_ge(silu_c, 1)

            def slot(l, i):
                pe.wait_ge(slot_loaded[i % RING], arrived(l, i))
                return ring[:, i % RING, :].rearrange("p (k n) -> p k n", k=KT)

            def turn(b, src):
                for j in range(4):
                    mm = pe.transpose(psum[:, b, j * P:(j + 1) * P], src[:, j * P:(j + 1) * P], ident)
                return mm

            def turn_x(l, sub):
                pe.wait_ge(x_ready, l * 2 + (sub + 1))
                for g in range(G):
                    for b in range(2):
                        turn(2 * g + b, x[:, g, b * W:(b + 1) * W]).then_inc(xt_filled, 1)
                pe.wait_ge(xt_read, l * 8 + (4 * sub + 4))

            def gate_row(l, sub, half_, g):
                n = 4 * sub + 2 * half_ + g
                if n in (0, 1):
                    pe.wait_ge(yt_ready, l * 4 + 4)
                elif n == 4:
                    pe.wait_ge(xg_ready, step(l, PASSES, 0))
                elif n == 5:
                    pe.wait_ge(eout_ready, step(l, PASSES, 0))
                else:
                    pe.wait_ge(grep_ready, l * 8 + (n - 1))
                pe.matmul(bank(4 + n % 2), ident[0:8, n:n + 1].to_broadcast([8, P]), grow[:, :], start=True, stop=True).then_inc(grep_filled, 1)

            with pe.Fori(0, DEPTH) as l:
                pe.wait_ge(ldata_loaded, l * 32 + 32)

                def h_round(n):
                    kind, g, i = H_ROUNDS[n]
                    if n:
                        pe.wait_ge(h_act, l * NH + n)
                        pe.wait_ge(h_dve, l * NH + n)
                        pe.wait_ge(h_pool, l * NH + n)
                    if kind in ("prep", "gate"):
                        pe.sem_inc(h_pe, 1)
                    if kind == "turn":
                        turn(EX, ch[:, g, CQ, :])
                        turn(EX + 1, ch[:, g, CF_F, :])
                        turn(PP, ch[:, g, CF_B, :]).then_inc(h_pe, 1)
                    if kind == "level":
                        for d in range(2 if i else 1):
                            for h in range(HEADS):
                                hp = slice(h * P, (h + 1) * P)
                                mm = pe.matmul(psum[:, PP + d, hp], k_dec[:, d, hp], q_dec[:, d, hp] if i else q_T[:, hp],
                                               start=True, stop=True)
                        mm.then_inc(h_scores, 1)
                        for d in range(2):
                            if i == NL and g == 0:
                                mm = pe.matmul(bank(EX + d), rest[d], log_f[:, d, :], start=True, stop=True)
                                continue
                            for h in range(HEADS):
                                mm = pe.matmul(psum[:, EX + d, h * P:(h + 1) * P], log_f[:, d, h * P:(h + 1) * P],
                                               level[d][:, i, :] if i < NL else tri[d], start=True, stop=True)
                        mm.then_inc(h_pe, 1)
                    if kind == "out":
                        pe.wait_ge(proj_read, proj(l, CI, g))
                        if g == 0:
                            for d in range(2):
                                for h in range(HEADS):
                                    hp = slice(h * P, (h + 1) * P)
                                    pe.matmul(psum[:, EX + d, hp], k_dec[:, d, hp], ch[:, g, CI, hp], start=True, stop=True)
                        for h in range(HEADS):
                            hp = slice(h * P, (h + 1) * P)
                            mm = pe.matmul(psum[:, PP, hp], att[:, hp], ch[:, g, CI, hp], start=True, stop=(g == 0))
                            if g == 1:
                                for d in range(2):
                                    mm = pe.matmul(psum[:, PP, hp], q_dec[:, d, hp], S0[:, d, h, :], start=False, stop=(d == 1))
                        mm.then_inc(h_pe, 1)

                def t_round(n):
                    kind, g, i = T_ROUNDS[n]
                    if n:
                        pe.wait_ge(t_act, l * NT + n)
                        pe.wait_ge(t_dve, l * NT + n)
                        pe.wait_ge(t_pool, l * NT + n)
                    if (kind, g) in T_CHUNK:
                        pe.wait_ge(proj_read, proj(l, T_CHUNK[kind, g], g))
                    mm = None
                    tiles = [slice(h * P, (h + 1) * P) for h in range(HEADS)]
                    if kind == "forget":
                        for gg in range(G):
                            for k in range(KT):
                                mm = pe.matmul(psum[:, T, gg * 16:gg * 16 + 16], hT[:, k, gg * P:(gg + 1) * P], w_gates[:, k, :],
                                               start=(k == 0), stop=(k == KT - 1))
                    if kind == "cumsum":
                        for d in range(2):
                            mm = pe.matmul(psum[:, T, d * 8:d * 8 + 8], tri[d], lf[:, d, :, :].rearrange("p g h -> p (g h)"),
                                           start=True, stop=True)
                    if kind in ("max", "decay"):
                        for d in range(2):
                            mm = pe.matmul(bank(T + d), ones, dg[:, d, :], start=True, stop=True)
                    if kind == "turn":
                        turn(T, ch[:, g, AQ, :])
                        mm = turn(T + 1, ch[:, g, AK, :])
                    if kind == "scores":
                        for hp in tiles:
                            mm = pe.matmul(psum[:, T, hp], kTa[:, hp], qTa[:, hp], start=True, stop=True)
                    if kind == "read_f":
                        for j in range(8):
                            pe.matmul(psum[:, T + 1, j:j + 1], em[:, j // 4, tiles[j % 4]], ones[:, 0:1], start=True, stop=True)
                            if g == 1:
                                pe.matmul(psum[:, T + 1, 8 + j:9 + j], qTa[:, tiles[j % 4]], l_("n0")[:, j:j + 1], start=True, stop=True)
                        for hp in tiles:
                            mm = pe.matmul(psum[:, T, hp], em[:, 0, hp], ch[:, g, AV, hp], start=True, stop=True)
                    if kind == "read_b":
                        for h, hp in enumerate(tiles):
                            mm = pe.matmul(psum[:, T, hp], em[:, 1, hp], ch[:, g, AV, hp], start=True, stop=True)
                        if g == 1:
                            for h, hp in enumerate(tiles):
                                mm = pe.matmul(psum[:, T + 1, hp], qTa[:, hp], C0[:, 0, h, :], start=True, stop=True)
                    if kind == "inter_b":
                        for h, hp in enumerate(tiles):
                            mm = pe.matmul(psum[:, T, hp], qTa[:, hp], C0[:, 1, h, :], start=True, stop=True)
                    if kind == "state":
                        for d in range(2):
                            for hp in tiles:
                                mm = pe.matmul(psum[:, T + d, hp], dg[:, d, hp], ch[:, 0, AV, hp], start=True, stop=True)
                    if kind == "norm_state":
                        for d in range(2):
                            mm = pe.matmul(psum[0:1, T + d, :], ones[:, 0:1], dg[:, d, :], start=True, stop=True)
                    if kind == "na_turn":
                        turn(T, ch[:, g, BQ, :])
                        mm = turn(T + 1, ch[:, g, BK, :])
                    if kind == "na_cache":
                        mm = turn(T, l_("ck"))
                    if kind == "na_scores":
                        o = NAD * i
                        for jp in tiles:
                            mm = pe.matmul(psum[:, T, jp], na_qT[o:o + NAD, jp], na_kT[o:o + NAD, jp], start=True, stop=True)
                        if g == 1:
                            for jp in tiles:
                                mm = pe.matmul(psum[:, T + 1, jp], na_qT[o:o + NAD, jp], na_cT[o:o + NAD, jp], start=True, stop=True)
                    if kind == "na_probs":
                        mm = turn(T, na_s[:, 0, :])
                        if g == 1:
                            mm = turn(T + 1, na_s[:, 1, :])
                    if kind == "na_out":
                        for j, jp in enumerate(tiles):
                            hc = slice((2 * j + i) * NAD, (2 * j + i + 1) * NAD)
                            o = psum[:, T, j * NAD:(j + 1) * NAD]
                            mm = pe.matmul(o, na_pT[:, 0, jp], ch[:, g, BV, hc], start=True, stop=(g == 0))
                            if g == 1:
                                mm = pe.matmul(o, na_pT[:, 1, jp], l_("cv")[:, hc], start=False, stop=True)
                    if mm is None:
                        pe.sem_inc(t_pe, 1)
                    else:
                        mm.then_inc(t_pe, 1)

                n = 0
                for c in range(N_MOD):
                    w = slot(l, c)
                    if c in MOD_COLS:
                        for j in range(4):
                            o = psum[:, T, (MOD_COLS[c] + j) * G:(MOD_COLS[c] + j + 1) * G]
                            for k in range(KT):
                                mm = pe.matmul(o, w[:, k, j * P:(j + 1) * P], scT[:, k, :], start=(k == 0), stop=(k == KT - 1))
                    else:
                        for k in range(KT):
                            mm = pe.matmul(psum[0:8, T + 1, :], scZ[:, k, MOD_ROWS[c], :], w[:, k, :],
                                           start=(n == 0), stop=(n == 4 * KT - 1))
                            n += 1
                    mm.then_inc(slot_used, 1)
                turn_x(l, 0)
                for q in range(QUARTERS):
                    in_order(h_round, t_round, q)
                    c, g, part = q // 4, (q // 2) % 2, q % 2
                    w = slot(l, N_MOD + c)
                    if part == 0 and c:
                        pe.wait_ge(proj_read, proj(l, c - 1, g))
                    for k in range(4 * part, 4 * part + 4):
                        mm = pe.matmul(bank(PJ + g), hT[:, k, g * P:(g + 1) * P], w[:, k, :], start=(k == 0), stop=(k == KT - 1))
                    if part:
                        mm.then_inc(slot_used if g else proj_filled, 1)
                pe.wait_ge(h_dve, l * NH + NH)
                pe.wait_ge(t_dve, l * NT + NT)
                pe.wait_ge(proj_read, proj(l, N_IN - 1, 1))
                for b, src in enumerate((AO, BQ, CG)):
                    if b:
                        pe.wait_ge(br_ready, l * 3 + b)
                    for g in range(G):
                        for k in range(BT):
                            mm = pe.transpose(psum[:, T + k // 2, (k % 2) * 256 + g * P:(k % 2) * 256 + (g + 1) * P],
                                              ch[:, g, src, k * P:(k + 1) * P], ident)
                    mm.then_inc(br_turned, 1)
                    w = ring[:, (N_MOD + N_IN + b) % RING, :].rearrange("p (k n) -> p k n", k=BT)
                    slot(l, N_MOD + N_IN + b)
                    pe.wait_ge(br_ready, l * 3 + (b + 1))
                    for g in range(G):
                        for hf in range(2):
                            if b:
                                pe.wait_ge(br_added, l * 12 + (4 * (b - 1) + 2 * g + hf + 1))
                            for k in range(BT):
                                mm = pe.matmul(bank(2 * g + hf), brT[:, b % 2, k, g * P:(g + 1) * P],
                                               w[:, k, hf * W:(hf + 1) * W], start=(k == 0), stop=(k == BT - 1))
                            mm.then_inc(slot_used if (g, hf) == (1, 1) else br_filled, 1)
                for g in range(G):
                    for b in range(2):
                        pe.wait_ge(br_added, l * 12 + (8 + 2 * g + b + 1))
                        turn(4 + 2 * g + b, y[:, g, b * W:(b + 1) * W]).then_inc(yt_filled, 1)
                pe.wait_ge(yt_ready, l * 4 + 4)
                for hf in range(2):
                    w = slot(l, N_MOD + N_IN + N_BR + hf)
                    for g in range(G):
                        gate_row(l, 0, hf, g)
                        if (hf, g) == (1, 1):
                            slot(l, FIRST_EXPERT_SLOT - 1)
                        for k in range(KT):
                            mm = pe.matmul(bank(2 * hf + g), hT[:, k, g * P:(g + 1) * P], w[:, k, :],
                                           start=(k == 0), stop=(k == KT - 1))
                        mm.then_inc(slot_used if g else out_filled, 1 + hf * g)
                turn_x(l, 1)
                for g in range(G):
                    for k in range(KT):
                        mm = pe.matmul(psum[:, T, g * 20:g * 20 + 20], hT[:, k, g * P:(g + 1) * P], w_route[:, k, :],
                                       start=(k == 0), stop=(k == KT - 1))
                mm.then_inc(rt_filled, 1)
                for g in range(G):
                    for b in range(2):
                        for j in range(4):
                            mm = pe.transpose(psum[:, 2 * g + b, j * P:(j + 1) * P], hT[:, 4 * b + j, g * P:(g + 1) * P], ident)
                        mm.then_inc(h2_turned, 1)
                pe.wait_ge(sent_ready, l + 1)
                flat = sent.rearrange("p g n -> p (g n)")
                pe.matmul(psum[:, T, 0:G * NE], rest[1], flat, start=True, stop=True)
                pe.matmul(psum[:, T, G * NE:2 * G * NE], ones, flat, start=True, stop=True).then_inc(ranked, 1)
                pe.wait_ge(h2_ready, l * 4 + 4)

                def w_up(j):
                    return ring[:, j, :].rearrange("p (k n) -> p k n", k=KT)

                w_down = ring[:, 2, :].rearrange("p (k n) -> p k n", k=BT)
                halves_of = [slice(0, CAP), slice(CAP, P)]

                def gather(n):
                    pe.wait_ge(pick_ready, n + 1)
                    for g in range(G):
                        for hf in range(2):
                            mm = pe.matmul(psum[halves_of[hf], 2, :], e_pick[:, g, :], h2tok[:, g, hf * W:(hf + 1) * W],
                                           start=(g == 0), stop=(g == 1))
                    mm.then_inc(gathered, 1)

                def turn_tokens(n):
                    pe.wait_ge(xs_ready, n + 1)
                    pe.wait_ge(xg_ready, n)
                    turn(4, xs).then_inc(xg_turned, 1)

                def up(j, p, e):
                    pe.wait_ge(slot_loaded[j], arrived_e(l, p, e))
                    for k in range(KT):
                        for hf in range(2):
                            mm = pe.matmul(psum[halves_of[hf], j, 0:FE // 2], xgT[:, k, :], w_up(j)[:, k, hf * (FE // 2):(hf + 1) * (FE // 2)],
                                           start=(k == 0), stop=(k == KT - 1))
                    mm.then_inc(slot_used, 1)

                def expert(p, e, last=False):
                    n = step(l, p, e)
                    up(1, p, e)
                    pe.wait_ge(sel_ready, n + 1)
                    pe.wait_ge(spread_added, n * 4)
                    for g in range(G):
                        mm = pe.transpose(psum[:, 3, g * P:(g + 1) * P], e_sel[:, g, :], ident)
                    mm.then_inc(sel_turned, 1)
                    if not last:
                        gather(n + 1)
                    pe.wait_ge(hid_ready, n + 1)
                    pe.wait_ge(eout_ready, n)
                    for j in range(2):
                        mm = pe.transpose(psum[:, 5, j * P:(j + 1) * P], ehid[:, j * P:(j + 1) * P], ident)
                    mm.then_inc(hid_turned, 1)
                    if not last:
                        turn_tokens(n + 1)
                    pe.wait_ge(hidT_ready, n + 1)
                    pe.wait_ge(slot_loaded[2], arrived_e(l, p, e))
                    for k in range(BT):
                        for hf in range(2):
                            mm = pe.matmul(psum[halves_of[hf], 5, :], ehidT[:, (k % 2) * P + (k // 2) * CAP:(k % 2) * P + (k // 2) * CAP + CAP],
                                           w_down[:, k, hf * W:(hf + 1) * W], start=(k == 0), stop=(k == BT - 1))
                    mm.then_inc(slot_used, 1)
                    if not last:
                        pe.wait_ge(xg_ready, n + 2)
                        up(0, p, e + 1)
                    pe.wait_ge(selT_ready, n + 1)
                    pe.wait_ge(eout_ready, n + 1)
                    for g in range(G):
                        for hf in range(2):
                            pe.matmul(bank(SPREAD[g][hf]), e_selT[halves_of[hf], g, :], e_out[halves_of[hf], :], start=True, stop=True)\
                              .then_inc(spread, 1)

                def expert_pass(p):
                    n = step(l, p, 0)
                    pe.wait_ge(spread_added, n * 4)
                    gather(n)
                    turn_tokens(n)
                    pe.wait_ge(xg_ready, n + 1)
                    up(0, p, 0)
                    with pe.Fori(0, NE - 1) as e:
                        expert(p, e)
                    expert(p, NE - 1, last=True)

                def no_pass(p):
                    pe.wait_ge(slot_used, used_e(l, p, 0, -1))
                    pe.sem_inc(slot_used, 3 * NE)
                    skip(pe, l, p, PE_STEP)

                expert_pass(0)
                further_passes(pe, l, expert_pass, no_pass)
                for hf in range(2):
                    for g in range(G):
                        gate_row(l, 1, hf, g)
                pe.wait_ge(spread_added, step(l, PASSES, 0) * 4)

        @block.scalar
        def _(act):
            credit(act, ACT_STEP)
            act.wait_ge(start_loaded, 48)
            act.activation(mod[:, 0:KT, :], scT[:, :, :], ACT.Exp, scale=-1.0).then_inc(exp_c, 1)

            with act.Fori(0, DEPTH) as l:
                link = Chain(act, act_chain, 16, l)
                act.wait_ge(lb_max, l + 1)
                act.activation(lb_e, lb_e, ACT.Exp).then_inc(lb_exp, 1)

                def h_round(n):
                    kind, g, i = H_ROUNDS[n]
                    act.wait_ge(h_pe, l * NH + (n + 1))
                    if kind == "prep":
                        act.wait_ge(proj_read, proj(l, CQ, g))
                        act.activation(hsig, ch[:, g, CF_F:CQ + 1, :].rearrange("p c n -> p (c n)"), ACT.Exp, scale=-1.0)\
                           .then_inc(h_exp, 1)
                        act.wait_ge(h_forget, l * G + (g + 1))
                        act.activation(log_f.rearrange("p d n -> p (d n)"), hsig[:, 0:2 * W], ACT.Ln).then_inc(h_act, 1)
                    elif kind == "turn":
                        act.activation(k_T[:, 0, :], bank(EX + 1), ACT.Copy)
                        act.activation(k_T[:, 1, :], bank(PP), ACT.Copy).then_inc(h_act, 1)
                    elif kind == "level":
                        act.activation(decay, bank(EX, 2), ACT.Exp).then_inc(h_act, 1)
                    elif kind == "out":
                        if g == 0:
                            link(act.activation(decay, bank(EX, 2), ACT.Copy))
                            act.dma_start(out["hgrn"][l].rearrange("d h k e -> k d h e"),
                                          decay.rearrange("p d (h n) -> p d h n", h=HEADS)).then_inc(hgrn_stored, 16)
                        act.wait_ge(h_square, l * G + (g + 1))
                        link(act.activation(h4b, h4, ACT.Ln))
                        if g == 0:
                            act.wait_ge(hgrn_stored, l * 16 + 16)
                        act.activation(h4b, h4b, ACT.Exp, scale=-0.5).then_inc(h_act, 1)
                    elif kind == "gate":
                        act.wait_ge(proj_read, proj(l, CG, g))
                        act.activation(hbuf[:, 0:W], ch[:, g, CG, :], ACT.Exp, scale=-1.0).then_inc(h_act, 1)

                def t_round(n):
                    kind, g, i = T_ROUNDS[n]
                    act.wait_ge(t_pe, l * NT + (n + 1))
                    if kind == "forget":
                        act.wait_ge(t_half, half(l, n, 0))
                        act.activation(fn, fn, ACT.Exp).then_inc(t_back, 1)
                        act.wait_ge(t_half, half(l, n, 1))
                        act.activation(fn, fn, ACT.Ln).then_inc(t_act, 1)
                    elif kind == "decay":
                        act.wait_ge(t_half, half(l, n))
                        act.wait_ge(t_pool, l * NT + n)
                        for d in range(2):
                            for h in range(HEADS):
                                hp = slice(h * P, (h + 1) * P)
                                act.activation(em[:, d, hp], em[:, d, hp], ACT.Exp, bias=ig[:, d, g, h:h + 1])
                        act.activation(wi[:, :, g, :], wi[:, :, g, :], ACT.Exp)
                        if g == 0:
                            act.activation(ws, ws, ACT.Exp)
                        act.activation(ex[:, :, g, :], mt[:, :, g, :], ACT.Exp, scale=-1.0).then_inc(t_act, 1)
                    elif kind == "turn":
                        act.activation(kTa, bank(T + 1), ACT.Copy, scale=QSCALE).then_inc(t_act, 1)
                    elif kind == "state":
                        link(act.activation(em, bank(T, 2), ACT.Copy))
                        act.dma_start(out["C"][l].rearrange("d h k e -> k d h e"),
                                      em.rearrange("p d (h n) -> p d h n", h=HEADS)).then_inc(state_stored, 16)
                        act.sem_inc(t_act, 1)
                    elif kind == "norm_state":
                        row = tbuf[0:1, 4 * W:6 * W]
                        link(act.activation(row.rearrange("p (b n) -> p b n", b=2), psum[0:1, T:T + 2, :], ACT.Copy))
                        act.dma_start(out["n"][l], row).then_inc(state_stored, 16)
                        act.dma_start(out["m"][l, 0:1, :], mt[P - 1:P, 0, 0, :]).then_inc(state_stored, 16)
                        act.dma_start(out["m"][l, 1:2, :], mt[0:1, 1, 0, :]).then_inc(state_stored, 16)
                        act.wait_ge(state_stored, l * N_STATE + N_STATE)
                        act.sem_inc(t_act, 1)
                    elif kind == "gate":
                        act.wait_ge(proj_read, proj(l, AO, g))
                        act.activation(am, ch[:, g, AO, :], ACT.Exp, scale=-1.0).then_inc(t_act, 1)
                    elif kind == "na_turn":
                        act.activation(na_qT, bank(T), ACT.Copy, scale=NSCALE).then_inc(t_act, 1)
                    elif kind == "na_scores":
                        act.wait_ge(t_half, half(l, n))
                        act.activation(tbuf[:, 0:(1 + g) * W], tbuf[:, 0:(1 + g) * W], ACT.Exp).then_inc(t_act, 1)
                    elif kind == "na_probs" and g == 1:
                        act.activation(na_pT[:, 1, :], bank(T + 1), ACT.Copy).then_inc(t_act, 1)
                    else:
                        act.sem_inc(t_act, 1)

                for q in range(QUARTERS):
                    in_order(h_round, t_round, q)
                    c, g = q // 4, (q // 2) % 2
                    if q in (4 * BK + 3, 4 * BV + 3):
                        which = "na_k" if c == BK else "na_v"
                        act.wait_ge(proj_read, proj(l, c, 0))
                        act.dma_start(out[which][l].rearrange("h t n -> t h n"),
                                      ch[:, 0, c, :].rearrange("p (h n) -> p h n", h=NAH)).then_inc(kv_stored, 16)
                    if q % 2 and c >= 12:
                        act.wait_ge(proj_read, proj(l, c, g))
                        act.wait_ge(sig_done, l * 12 + ((c - 12) * 2 + g + 1))
                        act.activation(sig, ch[:, g, GATE_BUF[c - 12], :], ACT.Exp, scale=-1.0).then_inc(sig_exp, 1)
                act.wait_ge(kv_stored, l * 32 + 32)
                for b in range(3):
                    act.wait_ge(br_turned, l * 3 + (b + 1))
                    if b == 2:
                        act.wait_ge(slot_used, used(l, N_MOD + N_IN))
                    act.activation(tbuf[:, (b % 2) * 1024:(b % 2) * 1024 + 1024].rearrange("p (b n) -> p b n", b=2),
                                   bank(T, 2), ACT.Copy).then_inc(br_ready, 1)
                for g in range(G):
                    for b in range(2):
                        act.wait_ge(yt_filled, l * 4 + (2 * g + b + 1))
                        act.activation(hT[:, 4 * b:4 * b + 4, g * P:(g + 1) * P],
                                       bank(4 + 2 * g + b).rearrange("p (k n) -> p k n", k=4), ACT.Copy).then_inc(yt_ready, 1)

                def finish(sub):
                    for n in range(4 * sub, 4 * sub + 4):
                        act.wait_ge(grep_filled, l * 8 + (n + 1))
                        act.wait_ge(out_added, l * 8 + (n + 1))
                        act.activation(grep, bank(4 + n % 2), ACT.Copy).then_inc(grep_ready, 1)
                    for g in range(G):
                        act.wait_ge(ln_var, l * 4 + (2 * sub + g + 1))
                        link(act.activation(rstd, rstd, ACT.Ln))
                        act.activation(rstd, rstd, ACT.Exp, scale=-0.5).then_inc(ln_rstd, 1)

                finish(0)
                for g in range(G):
                    for b in range(2):
                        act.wait_ge(h2_turned, l * 4 + (2 * g + b + 1))
                        act.activation(h2tok[:, g, b * W:(b + 1) * W], bank(2 * g + b), ACT.Copy).then_inc(h2_ready, 1)
                for i, v in enumerate((r_d, r_e)):
                    act.wait_ge(rt_half, l * 2 + (i + 1))
                    act.activation(v, v, ACT.Exp).then_inc(rt_exp, 1)

                def tokens_out(n):
                    act.wait_ge(gathered, n + 1)
                    act.wait_ge(xg_turned, n)
                    act.activation(xs, bank(2), ACT.Copy).then_inc(xs_ready, 1)

                def sigmoid_exp(n, p, e):
                    act.wait_ge(slot_used, used_e(l, p, e, 0))
                    act.wait_ge(hid_ready, n)
                    act.activation(esig, psum[:, 0, 0:FE // 2], ACT.Exp, scale=-1.0).then_inc(up_exp, 1)

                def expert(p, e, last=False):
                    n = step(l, p, e)
                    act.wait_ge(sel_turned, n + 1)
                    act.wait_ge(spread, n * 4)
                    act.activation(e_selT.rearrange("p g n -> p (g n)"), psum[:, 3, 0:G * P], ACT.Copy).then_inc(selT_ready, 1)
                    if not last:
                        tokens_out(n + 1)
                    act.wait_ge(hid_turned, n + 1)
                    act.activation(ehidT, psum[:, 5, 0:FE // 2], ACT.Copy).then_inc(hidT_ready, 1)
                    act.wait_ge(slot_used, used_e(l, p, e, 2))
                    act.activation(e_out, bank(5), ACT.Copy).then_inc(eout_ready, 1)
                    if not last:
                        sigmoid_exp(n + 1, p, e + 1)

                def expert_pass(p):
                    tokens_out(step(l, p, 0))
                    sigmoid_exp(step(l, p, 0), p, 0)
                    with act.Fori(0, NE - 1) as e:
                        expert(p, e)
                    expert(p, NE - 1, last=True)

                def no_pass(p):
                    skip(act, l, p, ACT_STEP)

                expert_pass(0)
                further_passes(act, l, expert_pass, no_pass)
                finish(1)
                link.close()

        @block.vector
        def _(dve):
            tt, ts, stt = dve.tensor_tensor, dve.tensor_scalar, dve.scalar_tensor_tensor
            dve.sem_inc(ldata_free, 1)
            dve.sem_inc(x_ready, 1)
            dve.sem_inc(proj_read, 2 * RING)
            dve.sem_inc(sig_done, 1)
            dve.sem_inc(out_added, 1)
            credit(dve, DVE_STEP)
            dve.wait_ge(start_loaded, 48)
            dve.memset(scZ[:, :, :, :], 0.0).then_inc(dve_tick, 1)
            dve.wait_ge(exp_c, 1)
            ts(mod[:, 0:KT, :], mod[:, 0:KT, :], 1.0, None, ALU.add).then_inc(dve_tick, 1)
            dve.wait_ge(dve_tick, 2)
            dve.reciprocal(mod[:, 0:KT, :], mod[:, 0:KT, :]).then_inc(dve_tick, 1)
            dve.wait_ge(dve_tick, 3)
            tt(scT[:, :, :], scT[:, :, :], mod[:, 0:KT, :], ALU.mult).then_inc(dve_tick, 1)
            dve.wait_ge(dve_tick, 4)
            for j in range(4):
                ins = dve.tensor_copy(scZ[:, :, j, 2 * j:2 * j + 2], scT[:, :, :])
            ins.then_inc(silu_c, 1)

            with dve.Fori(0, DEPTH) as l:
                link = Chain(dve, dve_chain, 300, l)
                dve.wait_ge(ldata_loaded, l * 32 + 32)
                if DEPTH == 2:
                    link(tt(lb_m, lb_e[:, :, 0, :], lb_e[:, :, 1, :], ALU.max))
                for j in range(DEPTH):
                    ins = tt(lb_e[:, :, j, :], lb_e[:, :, j, :], lb_m, ALU.subtract)
                ins.then_inc(lb_max, 1)
                dve.wait_ge(lb_exp, l + 1)
                link(tt(lb_m, lb_e[:, :, 0, :], lb_e[:, :, 1, :], ALU.add))
                link(dve.reciprocal(lb_m, lb_m))
                link(tt(lb_m, lb_m, lb_e[:, :, 1, :], ALU.mult))
                link(ts(lb[:, :, :], lb_m, l_("past")[:, 1:2], None, ALU.mult))
                dve.wait_ge(slot_used, used(l, N_MOD - 1))
                link(tt(mod[:, :, :], psum[:, T, 0:64].rearrange("p (n g) -> p n g", g=G),
                        l_("b_mod").unsqueeze(2).to_broadcast([P, 32, G]), ALU.add))
                link(ts(mod[:, 8:16, :], mod[:, 8:16, :], 1.0, None, ALU.add))
                link(ts(mod[:, 24:32, :], mod[:, 24:32, :], 1.0, None, ALU.add))
                link(tt(grow[:, :], psum[0:8, T + 1, :], l_("b_rows")[0:8, :], ALU.add))

                def modulate(sub):
                    for n in range(4):
                        dve.wait_ge(xt_filled, l * 8 + (4 * sub + n + 1))
                        g, b = n // 2, n % 2
                        for j in range(4):
                            k = 4 * b + j
                            ins = ts(hT[:, k, g * P:(g + 1) * P], psum[:, n, j * P:(j + 1) * P],
                                     mod[:, SCALE[sub] + k, g:g + 1], mod[:, SHIFT[sub] + k, g:g + 1], ALU.mult, ALU.add)
                        ins.then_inc(xt_read, 1)

                modulate(0)

                def h_round(n):
                    kind, g, i = H_ROUNDS[n]
                    dve.wait_ge(h_pe, l * NH + (n + 1))
                    if kind == "prep":
                        dve.wait_ge(h_exp, l * G + (g + 1))
                        link(ts(hsig, hsig, 1.0, None, ALU.add))
                        dve.reciprocal(hsig, hsig).then_inc(h_sigmoid, 1)
                        dve.wait_ge(h_sigmoid, l * G + (g + 1))
                        tt(ch[:, g, CQ, :], ch[:, g, CQ, :], hsig[:, 2 * W:3 * W], ALU.mult).then_inc(h_dve, 1)
                    elif kind == "turn":
                        dve.tensor_copy(q_T, bank(EX)).then_inc(h_dve, 1)
                    elif kind == "level":
                        dve.wait_ge(h_scores, l * (G * (NL + 1)) + (g * (NL + 1) + i + 1))
                        if i == 0:
                            link(tt(heads(att), heads(bank(PP)), over_heads(ident), ALU.mult))
                        else:
                            for d in range(2):
                                dve.sem_inc(dve_tick, 1)
                                link(dve.copy_predicated(heads(att), over_heads(level_mask[:, d, i - 1, :]), heads(bank(PP + d))))
                        dve.wait_ge(h_act, l * NH + (n + 1))
                        if i < NL or g == 1:
                            tt(q_dec, decay, q_T.unsqueeze(1).to_broadcast([P, 2, W]), ALU.mult).then_inc(h_dve, 1)
                        else:
                            dve.sem_inc(h_dve, 1)
                    elif kind == "out":
                        link(dve.tensor_copy(o_sb, bank(PP)))
                        link(tt(att, o_sb, o_sb, ALU.mult))
                        link(dve.tensor_reduce(h4, heads(att), X, ALU.add))
                        ts(h4, h4, 1.0 / DK, RMS_EPS, ALU.mult, ALU.add).then_inc(h_square, 1)
                        dve.wait_ge(h_act, l * NH + (n + 1))
                        tt(heads(o_norm[:, g, :]), heads(o_sb), over_cols(h4b), ALU.mult).then_inc(h_dve, 1)
                    elif kind == "gate":
                        s = hbuf[:, 0:W]
                        dve.wait_ge(h_act, l * NH + (n + 1))
                        link(ts(s, s, 1.0, None, ALU.add))
                        link(dve.reciprocal(s, s))
                        link(tt(s, s, ch[:, g, CG, :], ALU.mult))
                        tt(ch[:, g, CG, :], s, o_norm[:, g, :], ALU.mult).then_inc(h_dve, 1)

                def t_round(n):
                    kind, g, i = T_ROUNDS[n]
                    dve.wait_ge(t_pe, l * NT + (n + 1))
                    if kind == "forget":
                        z = psum[:, T, 0:32].rearrange("p (g d t h) -> p d g t h", g=G, d=2, t=2)
                        b = l_("b_gates").rearrange("p (d t h) -> p d t h", d=2, t=2)
                        fb = l_("fbias").rearrange("p (d h) -> p d h", d=2)
                        for d in range(2):
                            tt(ig[:, d, :, :], z[:, d, :, 0, :], b[:, d, 0, :].unsqueeze(1).to_broadcast([P, G, 4]), ALU.add)
                            link(tt(fz[:, d, :, :], z[:, d, :, 1, :], b[:, d, 1, :].unsqueeze(1).to_broadcast([P, G, 4]), ALU.add))
                            link(tt(fz[:, d, :, :], fz[:, d, :, :], fb[:, d, :].unsqueeze(1).to_broadcast([P, G, 4]), ALU.add))
                        link(ts(fn, fz, -1.0, None, ALU.mult))
                        tt(fn, fn, fz, ALU.min).then_inc(t_half, 1)
                        dve.wait_ge(t_back, l + 1)
                        ts(fn, fn, 1.0, None, ALU.add).then_inc(t_half, 1)
                        link(ts(fz, fz, 0.0, None, ALU.min))
                        dve.wait_ge(t_act, l * NT + (n + 1))
                        tt(lf, fz, fn, ALU.subtract).then_inc(t_dve, 1)
                    elif kind == "cumsum":
                        flat = [v.rearrange("p d g h -> p (d g h)") for v in (bc, ig)]
                        link(dve.tensor_copy(flat[0], psum[:, T, 0:16]))
                        tt(flat[1], flat[1], flat[0], ALU.subtract).then_inc(t_dve, 1)
                    elif kind == "max":
                        for d in range(2):
                            link(tt(heads(am), heads(bank(T + d)), over_heads(mask[d]), ALU.add))
                            link(dve.tensor_reduce(mx[:, d, g, :], heads(am), X, ALU.max))
                        tt(mx[:, :, g, :], mx[:, :, g, :], m0[:, :, g, :], ALU.max).then_inc(t_dve, 1)
                    elif kind == "decay":
                        for d in range(2):
                            ins = tt(heads(em[:, d, :]), over_heads(mask[1 - d]), heads(bank(T + d)), ALU.subtract)
                            if g == 0:
                                last = (P - 1) * (1 - d)
                                ins = tt(ws[:, d, :], ig[:, d, g, :], heads(bank(T + d))[:, :, last], ALU.subtract)
                        ins.then_inc(t_half, 1)
                        dve.wait_ge(t_act, l * NT + (n + 1))
                        dve.sem_inc(t_dve, 1)
                    elif kind == "turn":
                        dve.tensor_copy(qTa, bank(T)).then_inc(t_dve, 1)
                    elif kind == "scores":
                        for d in range(2):
                            ins = tt(em[:, d, :], em[:, d, :], bank(T), ALU.mult)
                        ins.then_inc(t_dve, 1)
                    elif kind == "read_f":
                        den = psum[:, T + 1, 0:8].rearrange("p (d h) -> p d h", d=2)
                        if g == 0:
                            link(dve.tensor_copy(dn, den))
                        else:
                            q_n = psum[:, T + 1, 8:16].rearrange("p (d h) -> p d h", d=2)
                            link(tt(dn, q_n, wi[:, :, g, :], ALU.mult))
                            link(tt(dn, den, dn, ALU.add))
                        link(ts(rr, dn, -1.0, None, ALU.mult))
                        link(tt(dn, dn, rr, ALU.max))
                        link(tt(dn, dn, ex[:, :, g, :], ALU.max))
                        link(dve.reciprocal(rr, dn))
                        if g == 1:
                            link(tt(wi[:, :, g, :], wi[:, :, g, :], rr, ALU.mult))
                        tt(heads(hs), heads(bank(T)), over_cols(rr[:, 0, :]), ALU.mult).then_inc(t_dve, 1)
                    elif kind in ("read_b", "inter_b"):
                        terms = [(T, rr[:, 1, :])] + [(T + 1, wi[:, 0, 1, :])] * g if kind == "read_b" else [(T, wi[:, 1, 1, :])]
                        for j, (b, s) in enumerate(terms):
                            link(tt(heads(am), heads(bank(b)), over_cols(s), ALU.mult))
                            ins = tt(hs, hs, am, ALU.add)
                            if j < len(terms) - 1:
                                link(ins)
                        ins.then_inc(t_dve, 1)
                    elif kind == "gate":
                        dve.wait_ge(t_act, l * NT + (n + 1))
                        link(ts(am, am, 1.0, None, ALU.add))
                        link(dve.reciprocal(am, am))
                        tt(ch[:, g, AO, :], am, hs, ALU.mult).then_inc(t_dve, 1)
                    elif kind == "na_turn":
                        dve.tensor_copy(na_kT, bank(T + 1)).then_inc(t_dve, 1)
                    elif kind == "na_cache":
                        dve.tensor_copy(na_cT, bank(T)).then_inc(t_dve, 1)
                    elif kind == "na_scores":
                        s = [heads(na_s[:, 0, :]), heads(na_s[:, 1, :])]
                        if g == 0:
                            link(dve.tensor_reduce(n_mx, heads(bank(T)), X, ALU.max))
                            tt(s[0], heads(bank(T)), over_cols(n_mx), ALU.subtract).then_inc(t_half, 1)
                        else:
                            dve.tensor_reduce(n_mb, heads(bank(T + 1)), X, ALU.max)
                            link(tt(s[0], heads(bank(T)), heads(rpb[:, i, :]), ALU.add))
                            link(dve.tensor_reduce(n_mx, s[0], X, ALU.max))
                            link(tt(n_mx, n_mx, n_mb, ALU.max))
                            tt(s[0], s[0], over_cols(n_mx), ALU.subtract)
                            tt(s[1], heads(bank(T + 1)), over_cols(n_mx), ALU.subtract).then_inc(t_half, 1)
                        dve.wait_ge(t_act, l * NT + (n + 1))
                        link(dve.tensor_reduce(n_sum[:, 0, :], s[0], X, ALU.add))
                        if g == 1:
                            link(dve.tensor_reduce(n_sum[:, 1, :], s[1], X, ALU.add))
                            link(tt(n_sum[:, 0, :], n_sum[:, 0, :], n_sum[:, 1, :], ALU.add))
                        dve.reciprocal(n_sum[:, 0, :], n_sum[:, 0, :]).then_inc(t_dve, 1)
                    elif kind == "na_probs":
                        dve.tensor_copy(na_pT[:, 0, :], bank(T)).then_inc(t_dve, 1)
                    elif kind == "na_out":
                        o = ch[:, g, BQ, :].rearrange("p (j a n) -> p j a n", j=4, a=2)[:, :, i, :]
                        tt(o, psum[:, T, 0:4 * NAD].rearrange("p (j n) -> p j n", j=4), over_cols(n_sum[:, 0, :], NAD), ALU.mult)\
                            .then_inc(t_dve, 1)
                    else:
                        dve.sem_inc(t_dve, 1)

                def sigmoid(m):
                    dve.wait_ge(sig_exp, l * 12 + (m + 1))
                    link(ts(sig, sig, 1.0, None, ALU.add))
                    dve.reciprocal(ch[:, m % 2, GATE_BUF[m // 2], :], sig).then_inc(sig_done, 1)

                for q in range(QUARTERS):
                    in_order(h_round, t_round, q)
                    c, g = q // 4, (q // 2) % 2
                    if q % 2:
                        if g:
                            dve.wait_ge(slot_used, used(l, N_MOD + c))
                        else:
                            dve.wait_ge(proj_filled, l * N_IN + (c + 1))
                            dve.wait_ge(bias_loaded[c % RING], l * (N_IN // RING * 16) + (c // RING + 1) * 16)
                        tt(ch[:, g, c if c < 12 else GATE_BUF[c - 12], :], bank(PJ + g), bias_ring[:, c % RING, :], ALU.add)\
                            .then_inc(proj_read, 1)
                        if c >= 12 and (c, g) != (12, 0):
                            sigmoid((c - 12) * 2 + g - 1)
                sigmoid(11)
                for b in range(3):
                    for g in range(G):
                        for hf in range(2):
                            n = 2 * g + hf
                            if n == 3:
                                dve.wait_ge(slot_used, used(l, N_MOD + N_IN + b))
                            else:
                                dve.wait_ge(br_filled, l * 9 + (3 * b + n + 1))
                            gate = ch[:, g, GATE_BUF[2 * b + hf], :]
                            yh = y[:, g, hf * W:(hf + 1) * W]
                            if b == 0:
                                tt(yh, bank(n), gate, ALU.mult).then_inc(br_added, 1)
                            else:
                                dve.wait_ge(br_added, l * 12 + (4 * b + n))
                                link(tt(lnt[:, 0, 0:W], bank(n), gate, ALU.mult))
                                tt(yh, yh, lnt[:, 0, 0:W], ALU.add).then_inc(br_added, 1)

                def finish(sub):
                    for hf in range(2):
                        for g in range(G):
                            n = 4 * sub + 2 * hf + g
                            dve.wait_ge(grep_ready, l * 8 + (n + 1))
                            if sub == 0:
                                if g:
                                    dve.wait_ge(slot_used, used(l, N_MOD + N_IN + N_BR + hf))
                                else:
                                    dve.wait_ge(out_filled, l * 2 + (hf + 1))
                                src = bank(2 * hf + g)
                            else:
                                src = y_moe[:, g, hf * W:(hf + 1) * W]
                            xh = x[:, g, hf * W:(hf + 1) * W]
                            dve.wait_ge(out_added, l * 8 + (n + 1))
                            link(tt(lnt[:, 0, 0:W], src, grep, ALU.mult))
                            stt(out=xh, in0=xh, scalar=ALPHA, in1=lnt[:, 0, 0:W], op0=ALU.mult, op1=ALU.add).then_inc(out_added, 1)
                    dve.wait_ge(out_added, l * 8 + (4 * sub + 5))
                    dve.wait_ge(ln_loaded, l * 32 + (16 * sub + 16))
                    for g in range(G):
                        for hf in range(2):
                            link(dve.bn_stats(bn6[:, hf, :], x[:, g, hf * W:(hf + 1) * W]), dve_tick)
                        link(dve.bn_aggr(bn2, bn6.rearrange("p a b -> p (a b)")))
                        ts(rstd, bn2[:, 1:2], LN_EPS, None, ALU.add).then_inc(ln_var, 1)
                        dve.wait_ge(ln_rstd, l * 4 + (2 * sub + g + 1))
                        link(ts(x[:, g, :], x[:, g, :], bn2[:, 0:1], rstd, ALU.subtract, ALU.mult))
                        link(tt(x[:, g, :], x[:, g, :], lnb[:, 0, :], ALU.mult))
                        ins = tt(x[:, g, :], x[:, g, :], lnb[:, 1, :], ALU.add)
                        if g:
                            ins.then_inc(x_ready, 1)
                        else:
                            link(ins)

                finish(0)
                modulate(1)
                dve.wait_ge(rt_filled, l + 1)
                link(dve.tensor_copy(lg.rearrange("p g n -> p (g n)"), psum[:, T, 0:40]))

                def first_max(sel, val, mx_):
                    link(dve.tensor_reduce(mx_, val, X, ALU.max))
                    link(tt(sel, val, mx_.unsqueeze(2).to_broadcast([P, G, 4]), ALU.is_equal))
                    link(dve.tensor_copy(r_pre, sel[:, :, 0]))
                    for j in range(1, 4):
                        link(dve.tensor_copy(r_w, sel[:, :, j]))
                        link(tt(sel[:, :, j], sel[:, :, j], r_pre, ALU.is_gt))
                        link(tt(r_pre, r_pre, r_w, ALU.max))

                first_max(r_sel, lg[:, :, 0:4], r_mx)
                tt(r_d, lg[:, :, 0:4], r_mx.unsqueeze(2).to_broadcast([P, G, 4]), ALU.subtract).then_inc(rt_half, 1)
                link(tt(r_x, lg[:, :, 4:20].rearrange("p g (a b) -> p g a b", a=4), r_sel.unsqueeze(3).to_broadcast([P, G, 4, 4]), ALU.mult))
                link(tt(r_le, r_x[:, :, 0, :], r_x[:, :, 1, :], ALU.add))
                link(tt(r_le, r_le, r_x[:, :, 2, :], ALU.add))
                link(tt(r_le, r_le, r_x[:, :, 3, :], ALU.add))
                first_max(r_o1, r_le, r_m1)
                link(stt(out=r_le, in0=r_o1, scalar=NEG, in1=r_le, op0=ALU.mult, op1=ALU.add))
                first_max(r_o2, r_le, r_m2)
                tt(r_e, r_m2, r_m1, ALU.subtract).then_inc(rt_half, 1)
                link(tt(r_in, r_o1, r_o2, ALU.add))
                for g in range(G):
                    ins = tt(sent[:, g, :].rearrange("p (a b) -> p a b", a=4), r_sel[:, g, :].unsqueeze(2).to_broadcast([P, 4, 4]),
                             r_in[:, g, :].unsqueeze(1).to_broadcast([P, 4, 4]), ALU.mult)
                ins.then_inc(sent_ready, 1)
                dve.wait_ge(sent_ready, l + 1)
                dve.wait_ge(rt_exp, l * 2 + 1)
                link(dve.tensor_reduce(r_p, r_d, X, ALU.add))
                link(dve.reciprocal(r_p, r_p))
                dve.wait_ge(rt_exp, l * 2 + 2)
                link(ts(r_w, r_e, 1.0, None, ALU.add))
                link(dve.reciprocal(r_w, r_w))
                link(tt(r_w, r_w, r_p, ALU.mult))
                link(tt(r_e, r_e, r_w, ALU.mult))
                link(tt(r_o1, r_o1, r_w.unsqueeze(2).to_broadcast([P, G, 4]), ALU.mult))
                link(tt(r_o2, r_o2, r_e.unsqueeze(2).to_broadcast([P, G, 4]), ALU.mult))
                link(tt(r_in, r_o1, r_o2, ALU.add))
                for g in range(G):
                    link(tt(gw[:, g, :].rearrange("p (a b) -> p a b", a=4), r_sel[:, g, :].unsqueeze(2).to_broadcast([P, 4, 4]),
                            r_in[:, g, :].unsqueeze(1).to_broadcast([P, 4, 4]), ALU.mult))
                link(dve.memset(y_moe, 0.0))
                dve.sem_inc(ldata_free, 1)
                dve.wait_ge(ranked, l + 1)
                sums = psum[:, T, 0:2 * G * NE].rearrange("p (a g n) -> p a g n", a=2, g=G)
                link(dve.tensor_copy(total, sums[:, 1, 0, :]))
                link(ts(rank, sums[:, 0, :, :], 1.0, None, ALU.add))
                link(tt(rank[:, 1, :], rank[:, 1, :], total, ALU.add))
                link(tt(rank, rank, sent, ALU.mult))
                link(ts(rank, rank, -1.0, None, ALU.add))
                link(tt(total, total, sums[:, 1, 1, :], ALU.add))
                link(dve.tensor_reduce(most, total, X, ALU.max))
                ts(fullest[:, :], most, 0.0, None, ALU.add).then_inc(fullest_ready, 1)
                def pick(n, e):
                    for g in range(G):
                        ins = ts(e_pick[:, g, :], c_("iota"), rank[:, g, bass.ds(e, 1)], None, ALU.is_equal)
                    ins.then_inc(pick_ready, 1)

                def select(n, e):
                    for g in range(G):
                        ins = ts(e_sel[:, g, :].rearrange("p (a n) -> p a n", a=2), c_("iota").unsqueeze(1).to_broadcast([P, 2, CAP]),
                                 rank[:, g, bass.ds(e, 1)], gw[:, g, bass.ds(e, 1)], ALU.is_equal, ALU.mult)
                    ins.then_inc(sel_ready, 1)

                def tokens_in(n):
                    dve.wait_ge(xg_turned, n + 1)
                    dve.tensor_copy(xgT.rearrange("p (h j) s -> p h j s", h=2), bank(4).rearrange("p (j h s) -> p h j s", j=4, h=2))\
                        .then_inc(xg_ready, 1)

                def silu(n):
                    mlink = Chain(dve, moe_chain, 3, n)
                    dve.wait_ge(up_exp, n + 1)
                    mlink(ts(esig, esig, 1.0, None, ALU.add))
                    mlink(dve.reciprocal(esig, esig))
                    mlink(tt(esig, esig, psum[:, 0, 0:FE // 2], ALU.mult))

                def expert(p, e, last=False):
                    n = step(l, p, e)
                    if not last:
                        dve.wait_ge(gathered, n + 1)
                        pick(n + 1, e + 1)
                    dve.wait_ge(slot_used, used_e(l, p, e, 1))
                    dve.wait_ge(hid_turned, n)
                    tt(ehid, esig, psum[:, 1, 0:FE // 2], ALU.mult).then_inc(hid_ready, 1)
                    if not last:
                        dve.wait_ge(sel_turned, n + 1)
                        select(n + 1, e + 1)
                        tokens_in(n + 1)
                        silu(n + 1)
                    for g in range(G):
                        for hf in range(2):
                            dve.wait_ge(spread, n * 4 + (2 * g + hf + 1))
                            yh = y_moe[:, g, hf * W:(hf + 1) * W]
                            tt(yh, yh, bank(SPREAD[g][hf]), ALU.add).then_inc(spread_added, 1)

                def expert_pass(p):
                    n = step(l, p, 0)
                    pick(n, 0)
                    select(n, 0)
                    tokens_in(n)
                    silu(n)
                    dve.sem_inc(dve_tick, 1)
                    with dve.Fori(0, NE - 1) as e:
                        expert(p, e)
                    expert(p, NE - 1, last=True)

                def next_pass(p):
                    ts(rank, rank, -float(CAP), None, ALU.add).then_inc(rank_moved, 1)
                    dve.wait_ge(rank_moved, l * (PASSES - 1) + p)
                    expert_pass(p)

                def no_pass(p):
                    dve.sem_inc(rank_moved, 1)
                    skip(dve, l, p, DVE_STEP)

                expert_pass(0)
                further_passes(dve, l, next_pass, no_pass)
                dve.wait_ge(spread_added, step(l, PASSES, 0) * 4)
                finish(1)
                dve.wait_ge(x_ready, l * 2 + 3)
                link.close()

        @block.gpsimd
        def _(pool):
            tt = pool.tensor_tensor
            pool.wait_ge(start_loaded, 48)
            with pool.Fori(0, DEPTH) as l:
                link = Chain(pool, pool_chain, 64, l)
                pool.wait_ge(ldata_loaded, l * 32 + 32)

                def h_round(n):
                    kind, g, i = H_ROUNDS[n]
                    pool.wait_ge(h_pe, l * NH + (n + 1))
                    if kind == "prep":
                        pool.wait_ge(h_sigmoid, l * G + (g + 1))
                        s, t = decay, k_dec
                        link(tt(t, s, lb[:, :, :], ALU.mult))
                        link(tt(s, s, t, ALU.subtract))
                        link(tt(s, s, lb[:, :, :], ALU.add), pool_tick)
                        pool.tensor_scalar(ch[:, g, CF_F:CF_B + 1, :], s, -1.0, 1.0, ALU.mult, ALU.add)
                        link(pool.tensor_scalar(t, s, TINY, None, ALU.max), pool_tick)
                        pool.tensor_copy(s, t).then_inc(h_forget, 1)
                        pool.wait_ge(h_act, l * NH + (n + 1))
                        pool.sem_inc(h_pool, 1)
                    elif kind == "turn":
                        pool.wait_ge(h_act, l * NH + (n + 1))
                        tt(k_dec[:, 0, :], k_T[:, 0, :], k_T[:, 1, :], ALU.add).then_inc(h_pool, 1)
                    elif kind == "level":
                        pool.wait_ge(h_act, l * NH + (n + 1))
                        if i < NL:
                            tt(k_dec, k_T, decay, ALU.mult).then_inc(h_pool, 1)
                        elif g == 0:
                            tt(k_dec, ch[:, 0, CF_F:CF_B + 1, :], decay, ALU.mult).then_inc(h_pool, 1)
                        else:
                            pool.sem_inc(h_pool, 1)
                    else:
                        pool.sem_inc(h_pool, 1)

                def diagonal(v, g):
                    for d in range(2):
                        ins = tt(heads(dg[:, d, :]), over_heads(ident), over_cols(v[:, d, g, :]), ALU.mult)
                    return ins

                def t_round(n):
                    kind, g, i = T_ROUNDS[n]
                    pool.wait_ge(t_pe, l * NT + (n + 1))
                    nxt = T_ROUNDS[n + 1] if n + 1 < NT else None
                    if nxt and nxt[0] == "max":
                        pool.wait_ge(t_dve, l * NT + (n + 1))
                        diagonal(ig, nxt[1]).then_inc(t_pool, 1)
                    elif kind == "max":
                        pool.wait_ge(t_dve, l * NT + (n + 1))
                        tt(mt[:, :, g, :], bc[:, :, g, :], mx[:, :, g, :], ALU.add)
                        tt(wi[:, :, g, :], m0[:, :, g, :], mx[:, :, g, :], ALU.subtract)
                        diagonal(mx, g).then_inc(t_pool, 1)
                    elif kind == "decay" and g == 1:
                        pool.wait_ge(proj_read, proj(l, AK, 1))
                        halves_ = lambda v: v.rearrange("p (h a b n) -> p h a b n", h=4, a=2, b=2)
                        sin = c_("sin").rearrange("p (a b n) -> p a b n", a=2, b=2)
                        for c in (AQ, AK):
                            v = ch[:, 1, c, :]
                            tt(heads(am), heads(v), over_heads(c_("cos")), ALU.mult)
                            for b in range(2):
                                ins = tt(halves_(hs)[:, :, :, b, :], halves_(v)[:, :, :, 1 - b, :],
                                         sin[:, :, b, :].unsqueeze(1).to_broadcast([P, 4, 2, 32]), ALU.mult)
                            link(ins)
                            ins = tt(v, am, hs, ALU.add)
                            if c == AQ:
                                link(ins)
                        ins.then_inc(t_pool, 1)
                    elif kind == "read_b" and g == 0:
                        pool.sem_inc(pool_tick, 1)
                        link(pool.tensor_scalar(ws, ws, QSCALE, None, ALU.mult))
                        for d in range(2):
                            ins = tt(heads(dg[:, d, :]), heads(ch[:, 0, AK, :]), over_cols(ws[:, d, :]), ALU.mult)
                        ins.then_inc(t_pool, 1)
                    else:
                        pool.sem_inc(t_pool, 1)

                for q in range(QUARTERS):
                    in_order(h_round, t_round, q)
                link.close()


def constants():
    i = np.arange(P)
    c = np.zeros((P, N_CONST), np.float32)

    def put(name, v):
        a, n = CONST[name]
        c[:, a:a + n] = np.asarray(v, np.float32).reshape(P, n)

    row, col = i[:, None], i[None, :]
    put("ident", row == col)
    put("ones", np.ones((P, P)))
    put("tri_f", row <= col)
    put("tri_b", row >= col)
    put("rest_f", row > col)
    put("rest_b", row < col)
    put("below", np.where(col <= row, 0.0, NEG))
    put("above", np.where(col >= row, 0.0, NEG))
    lv = np.zeros((2, P, NL, P), np.float32)
    masks = np.zeros((P, 2, NL, P), np.uint8)
    for n, h in enumerate(LEVELS):
        mid = col // (2 * h) * (2 * h) + h
        right = col >= mid
        lv[0, :, n] = np.where(right, (row >= mid) & (row <= col), (row > col) & (row < mid))
        lv[1, :, n] = np.where(right, (row >= mid) & (row < col), (row >= col) & (row < mid))
        same = row // (2 * h) == col // (2 * h)
        masks[:, 0, n] = same & (row < mid) & (col >= mid)
        masks[:, 1, n] = same & (row >= mid) & (col < mid)
    put("level_mask", masks.reshape(P, -1).view(np.float32))
    put("level_f", lv[0])
    put("level_b", lv[1])
    quarter = DK // 4
    inv = (np.float32(10000.0) ** (-np.arange(0, DK // 2, 2, dtype=np.float32) / np.float32(DK // 2))).astype(np.float32)
    cos, sin = np.zeros((P, 2, 2, quarter), np.float32), np.zeros((P, 2, 2, quarter), np.float32)
    for a, pos in enumerate((i // GRID_W, i % GRID_W)):
        ang = pos.astype(np.float32)[:, None] * inv[None, :]
        cos[:, a, 0] = cos[:, a, 1] = np.cos(ang)
        sin[:, a, 0], sin[:, a, 1] = -np.sin(ang), np.sin(ang)
    put("iota", np.broadcast_to(np.arange(CAP), (P, CAP)))
    put("cos", cos)
    put("sin", sin)
    return c


def bias_index():
    t = np.arange(P)
    r, c = t // GRID_W, t % GRID_W
    start = np.clip(c - 8, 0, GRID_W - 16)
    inside = (c[None, :] >= start[:, None]) & (c[None, :] < start[:, None] + 16)
    dr = r[None, :] - r[:, None] + 7
    dc = np.clip(c[None, :] - c[:, None] + 15, 0, 30)
    return np.where(inside, dr * 31 + dc, -1)


def kernel(**inputs):
    import concourse.bacc as bacc
    from concourse.bass_utils import run_bass_kernel_spmd

    v = {k: np.asarray(a) for k, a in inputs.items()}

    def tiles(w, k):
        return w.reshape(k, P, -1).transpose(1, 0, 2).reshape(P, -1)

    def rep(a):
        return np.broadcast_to(a.reshape(1, -1), (P, a.size))

    stream = np.zeros((DEPTH, SLOTS, P, SLOT), np.float32)
    b_in = np.zeros((DEPTH, N_IN, P, W), np.float32)
    ldata = np.zeros((DEPTH, P, N_LDATA), np.float32)
    ln = np.zeros((DEPTH, 2, P, 2, D), np.float32)
    where = bias_index()
    for l in range(DEPTH):
        for c in range(N_MOD):
            stream[l, c] = tiles(v["w_mod"][l][:, c * W:(c + 1) * W], KT)
        for c in range(N_IN):
            cols = slice(CHUNK_COL[c], CHUNK_COL[c] + W)
            stream[l, N_MOD + c] = tiles(v["w_in"][l][:, cols], KT)
            b_in[l, c] = rep(v["b_in"][l, cols])
        for b in range(N_BR):
            stream[l, N_MOD + N_IN + b] = tiles(v["w_branch"][l, b], BT)
        for b in range(N_OUT):
            stream[l, N_MOD + N_IN + N_BR + b] = tiles(v["w_out"][l][:, b * W:(b + 1) * W], KT)
        for e in range(NE):
            stream[l, FIRST_EXPERT_SLOT + 3 * e] = tiles(v["w_e1"][l, e], KT)
            stream[l, FIRST_EXPERT_SLOT + 3 * e + 1] = tiles(v["w_e3"][l, e], KT)
            stream[l, FIRST_EXPERT_SLOT + 3 * e + 2] = tiles(v["w_e2"][l, e], BT)

        def put(name, a):
            at, n = LDATA[name]
            ldata[l, :a.shape[0], at:at + n] = a.reshape(a.shape[0], n)

        put("C0", v["state_mlstm_C"][0, l].transpose(2, 0, 1, 3))
        put("S0", v["state_hgrn"][0, l].transpose(2, 0, 1, 3))
        bias = v["na_rpb"][l].reshape(NAH, -1)[:, np.maximum(where, 0)]
        bias = np.where(where[None] >= 0, bias, np.float32(NEG))
        put("rpb", bias.reshape(4, 2, P, P).transpose(2, 1, 0, 3))
        put("ck", v["cache_na_k"][0, l].transpose(1, 0, 2))
        put("cv", v["cache_na_v"][0, l].transpose(1, 0, 2))
        gates = slice(GATES_COL, GATES_COL + 16)
        put("w_gates", tiles(v["w_in"][l][:, gates], KT))
        put("w_route", tiles(np.concatenate([v["w_rg"][l], v["w_re"][l]], 1), KT))
        put("b_gates", rep(v["b_in"][l, gates]))
        put("fbias", rep(v["mlstm_fbias"][l]))
        put("n0", v["state_mlstm_n"][0, l].transpose(2, 0, 1))
        m0 = np.zeros((P, 2, G, 4), np.float32)
        m0[:, :, 1, :] = v["state_mlstm_m"][0, l][None]
        put("m0", m0)
        bm = v["b_mod"][l].reshape(6, 2, 4, P)
        put("b_mod", np.concatenate([bm[s].reshape(8, P) for s in (0, 1, 3, 4)]).T)
        rows = np.zeros((8, W), np.float32)
        for s, vec in enumerate((2, 5)):
            for hf in range(2):
                rows[4 * s + 2 * hf:4 * s + 2 * hf + 2] = bm[vec, hf].reshape(1, W)
        put("b_rows", rows)
        past = np.zeros((P, DEPTH), np.float32)
        past[:, 1:l + 1] = 1.0
        put("past", past)
        for s in range(2):
            ln[l, s, :, 0] = v["ln_g"][l, s]
            ln[l, s, :, 1] = v["ln_b"][l, s]
    const = constants()
    arrays = {
        "const": const,
        "x": np.stack([v["x_prompt"][0], v["x_sample"][0]], 1),
        "c_cols": np.stack([v["c_ctx"].reshape(KT, P), v["c"][0].reshape(KT, P)], 2).transpose(1, 0, 2),
        "stream": stream.reshape(DEPTH * SLOTS, P, SLOT),
        "b_in": b_in.reshape(DEPTH * N_IN, P, W),
        "ldata": ldata,
        "ln": ln.reshape(DEPTH * 2, P, 2, D),
        "lb_logits": np.broadcast_to(v["hgrn_lb_logits"][None], (P, 2, DEPTH, W)),
    }
    arrays = {f"in_{k}": np.ascontiguousarray(a) for k, a in arrays.items()}
    outs = {"y": (G, P, D), "na_k": (DEPTH, NAH, P, NAD), "na_v": (DEPTH, NAH, P, NAD), "C": (DEPTH, 2, HEADS, DK, DK),
            "n": (DEPTH, 1, 2 * HEADS * DK), "m": (DEPTH, 2, HEADS), "hgrn": (DEPTH, 2, HEADS, DK, DK)}
    nc = bacc.Bacc("TRN2", target_bir_lowering=False, num_devices=1)
    dram = {k[3:]: nc.dram_tensor(k, a.shape, mybir.dt.from_np(a.dtype), kind="ExternalInput").ap() for k, a in arrays.items()}
    out = {k: nc.dram_tensor(f"out_{k}", s, F32, kind="ExternalOutput").ap() for k, s in outs.items()}
    build(nc, dram, out)
    r = run_bass_kernel_spmd(nc, [arrays], core_ids=[0]).results[0]
    r = {k: r[f"out_{k}"] for k in outs}
    return (r["y"][0][None], r["y"][1][None], r["na_k"][None], r["na_v"][None], r["C"][None],
            r["n"].reshape(1, DEPTH, 2, HEADS, DK), r["m"][None], r["hgrn"][None])
```
